# Optimizing a Trainium2 kernel written in Bass

```python
import jax
import jax.numpy as jnp
from jax import lax
import numpy as np

D_MODEL = 1024
BATCH = 1
SEQ = 256
DEPTH = 1

BRANCH_WIDTH = 512
N_BRANCH = 4
GDN_HEADS = 4
GDN_DK = 128
GDN_DV = 128
GDN_CONV = 4
GDN_CHUNK = 64
GDN_QK = GDN_HEADS * GDN_DK
GDN_V = GDN_HEADS * GDN_DV
CONF_WIDTH = BRANCH_WIDTH
CONF_KERNEL = 31
GMLP_WIDTH = BRANCH_WIDTH
GMLP_GROUPS = 4
GMLP_CHUNK = 128
SC_WIDTH = BRANCH_WIDTH
SC_KERNEL = 3
MOE_GROUPS = 8
MOE_PER_GROUP = 8
N_EXPERTS = MOE_GROUPS * MOE_PER_GROUP
MOE_TOPK = 2
D_EXPERT = 512
MOE_BLOCK = 256
EPS = 1e-6

SPLIT_SIZES = (GDN_QK, GDN_QK, GDN_V, GDN_V, GDN_HEADS, GDN_HEADS,
               2 * CONF_WIDTH, 2 * GMLP_WIDTH, 3 * SC_WIDTH, N_BRANCH * D_MODEL)
SPLIT_POINTS = tuple(int(p) for p in np.cumsum(SPLIT_SIZES)[:-1])
D_IN = int(sum(SPLIT_SIZES))

kernel_name = 'hybrid_gated_parallel_mixers_hier_moe'

def rmsnorm(x, w):
    xf = x.astype(jnp.float32)
    y = xf * lax.rsqrt(jnp.mean(xf * xf, -1, keepdims=True) + EPS)
    return (y * w.astype(jnp.float32)).astype(x.dtype)

def layernorm(x, w, b):
    xf = x.astype(jnp.float32)
    xc = xf - jnp.mean(xf, -1, keepdims=True)
    y = xc * lax.rsqrt(jnp.mean(xc * xc, -1, keepdims=True) + EPS)
    return (y * w.astype(jnp.float32) + b.astype(jnp.float32)).astype(x.dtype)

def l2norm(t):
    return t * lax.rsqrt(jnp.sum(t * t, -1, keepdims=True) + EPS)

def causal_dwconv(x, w):
    k_w, ch = w.shape
    return lax.conv_general_dilated(
        x, w[:, None, :].astype(x.dtype), window_strides=(1,), padding=[(k_w - 1, 0)],
        dimension_numbers=('NWC', 'WIO', 'NWC'), feature_group_count=ch)

def gated_delta_rule(q, k, v, g, beta):
    bsz, nh, t_len, dk = q.shape
    dv = v.shape[-1]
    c = GDN_CHUNK
    n = t_len // c
    q = q.reshape(bsz, nh, n, c, dk)
    k = k.reshape(bsz, nh, n, c, dk)
    v = v.reshape(bsz, nh, n, c, dv)
    g = jnp.cumsum(g.reshape(bsz, nh, n, c), axis=-1)
    beta = beta.reshape(bsz, nh, n, c)
    tril = jnp.tril(jnp.ones((c, c), bool))
    strict = jnp.tril(jnp.ones((c, c), bool), -1)
    diff = g[..., :, None] - g[..., None, :]
    decay = jnp.where(tril, jnp.exp(jnp.where(tril, diff, 0.0)), 0.0)
    k_beta = k * beta[..., None]
    v_beta = v * beta[..., None]
    lower = jnp.einsum('bhnid,bhnjd->bhnij', k_beta, k) * decay
    m = jnp.where(strict, lower, 0.0) + jnp.eye(c, dtype=q.dtype)
    u = lax.linalg.triangular_solve(m, v_beta, left_side=True, lower=True, unit_diagonal=True)
    w = lax.linalg.triangular_solve(m, k_beta * jnp.exp(g)[..., None], left_side=True,
                                    lower=True, unit_diagonal=True)
    attn = jnp.einsum('bhnid,bhnjd->bhnij', q, k) * decay
    q_dec = q * jnp.exp(g)[..., None]
    g_last = g[..., -1]
    k_dec = k * jnp.exp(g_last[..., None] - g)[..., None]

    def step(s, xs):
        qd, kd, uc, wc, ac, gl = xs
        v_new = uc - jnp.einsum('bhcd,bhde->bhce', wc, s)
        o = jnp.einsum('bhcd,bhde->bhce', qd, s) + jnp.einsum('bhij,bhje->bhie', ac, v_new)
        s = s * jnp.exp(gl)[..., None, None] + jnp.einsum('bhcd,bhce->bhde', kd, v_new)
        return s, o

    xs = tuple(jnp.moveaxis(t, 2, 0) for t in (q_dec, k_dec, u, w, attn, g_last))
    s0 = jnp.zeros((bsz, nh, dk, dv), jnp.float32)
    _, o = lax.scan(step, s0, xs)
    return jnp.moveaxis(o, 0, 2).reshape(bsz, nh, t_len, dv)

def gdn_branch(q, k, v, z, beta_raw, a_raw, conv_w, a_log, dt_bias, norm_w):
    bsz, t_len, _ = q.shape
    dtype = q.dtype
    qkv = jax.nn.silu(causal_dwconv(jnp.concatenate([q, k, v], -1), conv_w))
    q, k, v = jnp.split(qkv, [GDN_QK, 2 * GDN_QK], -1)

    def heads(t, d):
        return t.reshape(bsz, t_len, GDN_HEADS, d).transpose(0, 2, 1, 3).astype(jnp.float32)

    q = l2norm(heads(q, GDN_DK)) * (GDN_DK ** -0.5)
    k = l2norm(heads(k, GDN_DK))
    v = heads(v, GDN_DV)
    beta = jax.nn.sigmoid(beta_raw.astype(jnp.float32)).transpose(0, 2, 1)
    g = -jnp.exp(a_log.astype(jnp.float32)) * jax.nn.softplus(
        a_raw.astype(jnp.float32) + dt_bias.astype(jnp.float32))
    g = g.transpose(0, 2, 1)
    o = gated_delta_rule(q, k, v, g, beta).transpose(0, 2, 1, 3)
    o = o * lax.rsqrt(jnp.mean(o * o, -1, keepdims=True) + EPS) * norm_w.astype(jnp.float32)
    o = o * jax.nn.silu(z.reshape(bsz, t_len, GDN_HEADS, GDN_DV).astype(jnp.float32))
    return o.reshape(bsz, t_len, GDN_V).astype(dtype)

def conformer_branch(h, conv_w, conv_b, ln_w, ln_b):
    a, gate = jnp.split(h, 2, -1)
    y = a * jax.nn.sigmoid(gate)
    y = causal_dwconv(y, conv_w) + conv_b.astype(h.dtype)
    return jax.nn.silu(layernorm(y, ln_w, ln_b))

def gmlp_branch(h, ln_w, ln_b, w_s, b_s):
    bsz, t_len, _ = h.shape
    u, v = jnp.split(jax.nn.gelu(h), 2, -1)
    v = layernorm(v, ln_w, ln_b)
    n = t_len // GMLP_CHUNK
    gc = GMLP_WIDTH // GMLP_GROUPS
    v = v.reshape(bsz, n, GMLP_CHUNK, GMLP_GROUPS, gc)
    mask = jnp.tril(jnp.ones((GMLP_CHUNK, GMLP_CHUNK), bool))
    w_c = jnp.where(mask[None], w_s, 0.0).astype(h.dtype)
    mixed = jnp.einsum('gij,bnjgc->bnigc', w_c, v) + b_s.T.astype(h.dtype)[None, None, :, :, None]
    return u * mixed.reshape(bsz, t_len, GMLP_WIDTH)

def shortconv_branch(h, conv_w):
    b_gate, c_gate, xin = jnp.split(h, 3, -1)
    return b_gate * causal_dwconv(c_gate * xin, conv_w)

def mixer_block(x, norm_w, w_in, gdn_conv_w, gdn_a_log, gdn_dt_bias, gdn_norm_w,
                conf_conv_w, conf_conv_b, conf_ln_w, conf_ln_b, gmlp_ln_w, gmlp_ln_b,
                gmlp_w_s, gmlp_b_s, sc_conv_w, w_branch, w_out):
    bsz, t_len, _ = x.shape
    xn = rmsnorm(x, norm_w)
    h = xn @ w_in
    q, k, v, z, beta_raw, a_raw, h_conf, h_gmlp, h_sc, h_gate = jnp.split(h, SPLIT_POINTS, -1)
    ys = (gdn_branch(q, k, v, z, beta_raw, a_raw, gdn_conv_w, gdn_a_log, gdn_dt_bias, gdn_norm_w),
          conformer_branch(h_conf, conf_conv_w, conf_conv_b, conf_ln_w, conf_ln_b),
          gmlp_branch(h_gmlp, gmlp_ln_w, gmlp_ln_b, gmlp_w_s, gmlp_b_s),
          shortconv_branch(h_sc, sc_conv_w))
    gates = jax.nn.sigmoid(h_gate.reshape(bsz, t_len, N_BRANCH, D_MODEL))
    merged = gates[..., 0, :] * (ys[0] @ w_branch[0])
    for i in range(1, N_BRANCH):
        merged = merged + gates[..., i, :] * (ys[i] @ w_branch[i])
    return merged @ w_out

def hier_moe(x, router_grp, router_exp, w_gate, w_up, w_down):
    bsz, t_len, d = x.shape
    xf = x.reshape(-1, d)
    n_tok = xf.shape[0]
    p_grp = jax.nn.softmax((xf @ router_grp).astype(jnp.float32), -1)
    grp = jnp.argmax(p_grp, -1).astype(jnp.int32)
    p_sel = jnp.take_along_axis(p_grp, grp[:, None], -1)
    logits = (xf @ router_exp).astype(jnp.float32).reshape(n_tok, MOE_GROUPS, MOE_PER_GROUP)
    logits_g = jnp.take_along_axis(logits, grp[:, None, None], 1)[:, 0]
    w_top, idx_top = lax.top_k(jax.nn.softmax(logits_g, -1), MOE_TOPK)
    w_top = w_top / jnp.sum(w_top, -1, keepdims=True) * p_sel
    expert = grp[:, None] * MOE_PER_GROUP + idx_top.astype(jnp.int32)
    n_assign = n_tok * MOE_TOPK
    e_flat = expert.reshape(-1)
    tok_flat = jnp.repeat(jnp.arange(n_tok, dtype=jnp.int32), MOE_TOPK)
    w_flat = w_top.reshape(-1)
    order = jnp.argsort(e_flat)
    e_sorted = e_flat[order]
    counts = jnp.zeros((N_EXPERTS,), jnp.int32).at[e_flat].add(1)
    padded = (counts + MOE_BLOCK - 1) // MOE_BLOCK * MOE_BLOCK
    pad_end = jnp.cumsum(padded)
    pad_start = pad_end - padded
    start = jnp.cumsum(counts) - counts
    dest = pad_start[e_sorted] + jnp.arange(n_assign, dtype=jnp.int32) - start[e_sorted]
    n_blocks = (n_assign + N_EXPERTS * (MOE_BLOCK - 1)) // MOE_BLOCK + 1
    n_rows = n_blocks * MOE_BLOCK
    buf_tok = jnp.full((n_rows,), n_tok, jnp.int32).at[dest].set(tok_flat[order])
    buf_w = jnp.zeros((n_rows,), jnp.float32).at[dest].set(w_flat[order])
    blk_start = jnp.arange(n_blocks, dtype=jnp.int32) * MOE_BLOCK
    blk_expert = jnp.minimum(jnp.searchsorted(pad_end, blk_start, side='right'),
                             N_EXPERTS - 1).astype(jnp.int32)
    x_pad = jnp.concatenate([xf, jnp.zeros((1, d), xf.dtype)], 0)

    def run_block(args):
        toks, e = args
        xb = x_pad[toks]
        hb = jax.nn.silu(xb @ w_gate[e]) * (xb @ w_up[e])
        return hb @ w_down[e]

    y = lax.map(run_block, (buf_tok.reshape(n_blocks, MOE_BLOCK), blk_expert))
    y = y.reshape(n_rows, d) * buf_w[:, None].astype(x.dtype)
    out = jnp.zeros((n_tok + 1, d), x.dtype).at[buf_tok].add(y)[:n_tok]
    return out.reshape(bsz, t_len, d)

def setup_inputs(seed: int = 0) -> dict:
    key = jax.random.key(seed)
    ks = jax.random.split(key, 26)
    f32 = jnp.float32
    L = DEPTH

    def nrm(k, shape, scale):
        return jax.random.normal(k, shape, f32) * scale

    def gain(k, shape):
        return 1.0 + 0.02 * jax.random.normal(k, shape, f32)

    dt = jnp.exp(jax.random.uniform(ks[4], (L, GDN_HEADS), f32, np.float32(np.log(1e-3)),
                                    np.float32(np.log(1e-1))))
    return {
        'x': nrm(ks[0], (BATCH, SEQ, D_MODEL), 1.0),
        'mix_norm_w': gain(ks[1], (L, D_MODEL)),
        'w_in': nrm(ks[2], (L, D_MODEL, D_IN), D_MODEL ** -0.5),
        'gdn_conv_w': nrm(ks[3], (L, GDN_CONV, 2 * GDN_QK + GDN_V), GDN_CONV ** -0.5),
        'gdn_A_log': jnp.log(jax.random.uniform(ks[5], (L, GDN_HEADS), f32, 1.0, 16.0)),
        'gdn_dt_bias': dt + jnp.log(-jnp.expm1(-dt)),
        'gdn_norm_w': gain(ks[6], (L, GDN_DV)),
        'conf_conv_w': nrm(ks[7], (L, CONF_KERNEL, CONF_WIDTH), CONF_KERNEL ** -0.5),
        'conf_conv_b': nrm(ks[8], (L, CONF_WIDTH), 0.02),
        'conf_ln_w': gain(ks[9], (L, CONF_WIDTH)),
        'conf_ln_b': nrm(ks[10], (L, CONF_WIDTH), 0.02),
        'gmlp_ln_w': gain(ks[11], (L, GMLP_WIDTH)),
        'gmlp_ln_b': nrm(ks[12], (L, GMLP_WIDTH), 0.02),
        'gmlp_w_s': nrm(ks[13], (L, GMLP_GROUPS, GMLP_CHUNK, GMLP_CHUNK), GMLP_CHUNK ** -0.5),
        'gmlp_b_s': gain(ks[14], (L, GMLP_GROUPS, GMLP_CHUNK)),
        'sc_conv_w': nrm(ks[15], (L, SC_KERNEL, SC_WIDTH), SC_KERNEL ** -0.5),
        'w_branch': nrm(ks[16], (L, N_BRANCH, BRANCH_WIDTH, D_MODEL), BRANCH_WIDTH ** -0.5),
        'w_out': nrm(ks[17], (L, D_MODEL, D_MODEL), D_MODEL ** -0.5),
        'moe_norm_w': gain(ks[18], (L, D_MODEL)),
        'router_grp': nrm(ks[19], (L, D_MODEL, MOE_GROUPS), D_MODEL ** -0.5),
        'router_exp': nrm(ks[20], (L, D_MODEL, N_EXPERTS), D_MODEL ** -0.5),
        'w_gate': nrm(ks[21], (L, N_EXPERTS, D_MODEL, D_EXPERT), D_MODEL ** -0.5),
        'w_up': nrm(ks[22], (L, N_EXPERTS, D_MODEL, D_EXPERT), D_MODEL ** -0.5),
        'w_down': nrm(ks[23], (L, N_EXPERTS, D_EXPERT, D_MODEL), D_EXPERT ** -0.5),
        'final_norm_w': gain(ks[24], (D_MODEL,)),
    }

def reference(x, mix_norm_w, w_in, gdn_conv_w, gdn_A_log, gdn_dt_bias, gdn_norm_w,
              conf_conv_w, conf_conv_b, conf_ln_w, conf_ln_b, gmlp_ln_w, gmlp_ln_b,
              gmlp_w_s, gmlp_b_s, sc_conv_w, w_branch, w_out, moe_norm_w, router_grp,
              router_exp, w_gate, w_up, w_down, final_norm_w):
    for l in range(DEPTH):
        x = x + mixer_block(x, mix_norm_w[l], w_in[l], gdn_conv_w[l], gdn_A_log[l],
                            gdn_dt_bias[l], gdn_norm_w[l], conf_conv_w[l], conf_conv_b[l],
                            conf_ln_w[l], conf_ln_b[l], gmlp_ln_w[l], gmlp_ln_b[l],
                            gmlp_w_s[l], gmlp_b_s[l], sc_conv_w[l], w_branch[l], w_out[l])
        x = x + hier_moe(rmsnorm(x, moe_norm_w[l]), router_grp[l], router_exp[l],
                         w_gate[l], w_up[l], w_down[l])
    return rmsnorm(x, final_norm_w)


_drawn_inputs = setup_inputs


def setup_inputs(seed=0):
    import zlib

    import numpy as np

    out = dict(_drawn_inputs(seed))
    spreads = {}
    factors = {'gdn_norm_w': 4.987,
     'conf_conv_b': 3.812,
     'conf_ln_w': 4.581,
     'conf_ln_b': 7.854,
     'gmlp_ln_w': 4.878,
     'gmlp_ln_b': 8.0,
     'gmlp_b_s': 5.589,
     'moe_norm_w': 2.756,
     'final_norm_w': 2.849}
    for name, (base, spread) in spreads.items():
        noise = np.random.default_rng([zlib.crc32(name.encode()), seed]).standard_normal(out[name].shape)
        drawn = base * np.exp(spread * noise) if base else spread * noise
        out[name] = jnp.asarray(drawn.astype(out[name].dtype))
    for name, factor in factors.items():
        out[name] = (out[name] * factor).astype(out[name].dtype)
    return out
```

```python
import concourse.bass as bass
from concourse import mybir
from contextlib import ExitStack


def hybrid_trunk_kernel(nc, x, mix_norm_w, w_in, gdn_conv_w, gdn_A_log, gdn_dt_bias, gdn_norm_w,
                        conf_conv_w, conf_conv_b, conf_ln_w, conf_ln_b, gmlp_ln_w, gmlp_ln_b,
                        gmlp_w_s, gmlp_b_s, sc_conv_w, w_branch, w_out, moe_norm_w, router_grp,
                        router_exp, w_gate, w_up, w_down, final_norm_w, out):
    f32 = mybir.dt.float32
    u32 = mybir.dt.uint32
    ALU = mybir.AluOpType
    ACT = mybir.ActivationFunctionType
    AXX = mybir.AxisListType.X

    P = 128
    _, SEQ, D = x.shape
    NT = SEQ // P
    KC = D // P
    BW = w_branch.shape[2]
    NCH = BW // P
    H = gdn_A_log.shape[1]
    CH = 64
    TAPS = gdn_conv_w.shape[1]
    CTAPS = conf_conv_w.shape[1]
    STAPS = sc_conv_w.shape[1]
    NG = router_grp.shape[2]
    NE = router_exp.shape[2]
    EG = NE // NG
    FE = w_gate.shape[3]
    FC = FE // P
    EPS = 1e-6
    EB = 4
    SL = P // EB
    NB = NE // EB
    HK = KC // 2
    PB = 2 * HK + FC

    R = 6
    PIECE = KC * BW

    OQ, OK, OV, OZ = 0, BW, 2 * BW, 3 * BW
    OAB = 4 * BW
    OCA = OAB + 2 * H
    OCG = OCA + BW
    OGU, OGV = OCG + BW, OCG + 2 * BW
    OSB, OSC, OSX = OGV + BW, OGV + 2 * BW, OGV + 3 * BW
    OG = OSX + BW

    def gate_cols(i, half):
        return ("in", OG + i * D + half * BW)

    FRONT = [("in", OK), ("in", OQ), ("in", OV), ("in", OCA), ("in", OCG),
             ("in", OSC), ("in", OSX), ("in", OSB), gate_cols(3, 0), gate_cols(3, 1), ("branch", 3),
             ("in", OGV), ("in", OGU), gate_cols(2, 0), gate_cols(2, 1), ("branch", 2),
             ("in", OZ), gate_cols(1, 0), gate_cols(1, 1), ("branch", 1),
             gate_cols(0, 0), gate_cols(0, 1), ("branch", 0), ("out", 0), ("out", BW)]
    (PK, PQ, PV, PCA, PCG, PSC, PSX, PSB, PG3A, PG3B, PW3, PGV, PGU, PG2A, PG2B, PW2,
     PZ, PG1A, PG1B, PW1, PG0A, PG0B, PW0, PO0, PO1) = range(len(FRONT))
    NF = len(FRONT)
    TOKEN_MAJOR = (PGV, PO0, PO1)
    EMPTIED_BY_ACT = (PK, PQ, PV, PCA, PCG, PSC, PG3A, PG3B, PG2A, PG2B, PG1A, PG1B, PG0A, PG0B)

    UNITS = [(m, h) for m in range(NF) for h in range(4 if FRONT[m][0] == "branch" else 2)]
    UNIT = {unit: u for u, unit in enumerate(UNITS)}

    def units_through(m):
        return sum(1 for unit in UNITS if unit[0] <= m)

    def bank_free(u):
        act = UNITS[u][0] in EMPTIED_BY_ACT
        count = sum(1 for v in range(u + 1) if (UNITS[v][0] in EMPTIED_BY_ACT) == act)
        return ("proj_taken_act" if act else "proj_taken_dve"), count

    ctx = ExitStack()
    with ctx:
        def sb(name, shape, dt=f32):
            return ctx.enter_context(nc.sbuf_tensor(name, shape, dt))

        ONCE = {
            "pe_steps": ["prm_done", "ws_done", "ab_done", "gc_done", "rows_done", "kf_done", "qf_done", "kb_done",
                         "vf_done", "KK_done", "qb_done", "qdb_done", "QK_done", "LT_done", "AT_done", "u_done",
                         "wT_done", "mix_done", "cfT_done", "oT_done", "cfB_done", "counts_done", "sum_closed"],
            "dve_steps": ["ss_ready", "prm_taken", "ws_taken", "abs_ready", "ab_taken", "g_ready", "k_conv",
                          "gc_taken", "decay_log", "k_act", "q_conv", "ssk_ready", "q_act", "kbg_ready", "v_conv",
                          "ssq_ready", "v_act", "qd_ready", "kd_ready", "L_ready", "A_masked", "A_ready"],
        }

        class Signals(dict):
            def __missing__(self, name):
                for counter, events in ONCE.items():
                    if name in events:
                        self[name] = self[counter]
                        return self[name]
                self[name] = ctx.enter_context(nc.semaphore(name))
                return self[name]

            def at(self, name, n):
                for events in ONCE.values():
                    if name in events:
                        return self[name], events.index(name) + 1
                return self[name], n

        S = Signals()

        ring = sb("ring", [P, R, PIECE])
        BLK = KC * P + 16
        NBLK = 20
        arena = sb("arena", [P, NBLK, BLK])
        conf_pad = sb("conf_pad", [P, NCH, CTAPS - 1 + SEQ])

        def blk(n, width=NCH * SEQ):
            return arena[:, n, 0:width]

        def cht(n):
            return blk(n).rearrange("p (c t) -> p c t", c=NCH)

        def tht(n):
            return blk(n).rearrange("p (t h d) -> p t h d", t=NT, h=H)

        def thf(n):
            return blk(n).rearrange("p (a d) -> p a d", d=P)

        def padded(n, pad):
            return blk(n, NCH * (pad + SEQ)).rearrange("p (c t) -> p c t", c=NCH)

        k_in, q_in, v_in = padded(0, TAPS - 1), padded(2, TAPS - 1), padded(4, TAPS - 1)
        k_ch, q_ch, v_ch = cht(1), cht(3), cht(5)
        k_tok, q_tok, vb_tok = tht(0), tht(2), tht(4)
        kbg_tok, qd_tok = tht(1), tht(3)
        kT, qT, qdT = tht(7), tht(8), tht(9)
        decay = tht(10)
        L_, QM, vn_tok = tht(11), tht(11), tht(11)
        Q_ = tht(12)
        A_, U_ = tht(13), tht(13)
        AT = tht(8)
        T_, V_ = tht(2), tht(3)
        u_tok = tht(5)
        wT = tht(7)
        o_tok = tht(10)
        x_sb = arena[:, 14:16, 0:D]
        xn = arena[:, 16:18, 0:D]
        xnT = sb("xnT", [P, KC, SEQ])
        state = sb("state", [P, H, P])
        conf_acc = cht(6)
        workA, workB = cht(14), cht(15)
        cx = padded(15, STAPS - 1)
        tan = [cht(16), cht(17)]
        merged = arena[:, 18:20, 0:NCH * SEQ].rearrange("p b (c t) -> p b c t", c=NCH)
        zbuf = cht(1)
        x_res = arena[:, 2:4, 0:D]
        ln_rows = blk(7).rearrange("p (n c) -> p n c", n=2)
        bs_row = blk(13)[:, 0:BW].rearrange("p (g i) -> p g i", g=H)
        g_wide = tht(17)
        cf_tok = tht(15)
        squares = thf(11)
        gm_v = arena[:, 14, 0:NT * BW].rearrange("p (t c) -> p t c", t=NT)
        gm_u = cht(15)

        ident = sb("ident", [P, P])
        ones = sb("ones", [P, P])
        up_incl = sb("up_incl", [P, P])
        lo_incl = sb("lo_incl", [P, P])
        lo_strict = sb("lo_strict", [P, P])
        same_chunk = sb("same_chunk", [P, P])
        NM = 6
        merge = sb("merge", [P, NM, P])
        merge_lo = sb("merge_lo", [P, P])
        prm = sb("prm", [P, NCH, 52])
        w_mix = sb("w_mix", [P, KC])
        w_abs = sb("w_abs", [P, KC, 2 * H])
        wcT = sb("wcT", [P, H, P])
        small = sb("small", [P, 256])
        NPRM = 3 * TAPS + CTAPS + STAPS + 3
        RQ, RK, RV = 0, TAPS, 2 * TAPS
        RC = 3 * TAPS
        RS = RC + CTAPS
        RCB = RS + STAPS
        RLW, RLB = RCB + 1, RCB + 2
        prm_rows = blk(13)[0:NPRM, 0:BW]
        ws_sb = blk(12)[:, 0:H * P].rearrange("p (g j) -> p g j", g=H)

        cursor = [0]

        def sm(n):
            a = cursor[0]
            cursor[0] += n
            return small[:, a:a + n]

        ss = sm(NT)
        rs = sm(NT)
        mhalf = sm(2 * NT * H)
        w_gn = sm(1)
        alog = sm(H)
        dtb = sm(H)
        expA = sm(H)
        beta = sm(NT * H)
        e1 = sm(NT * H)
        e2 = sm(NT * H)
        e3 = sm(NT * H)
        gl = sm(NT * H)
        egc = sm(NT * H)
        gcum = sm(NT * H)
        ekd = sm(NT * H)
        bgk = sm(NT * H)
        egl = sm(2 * NT * H)
        ssk, rk = sm(NT * H), sm(NT * H)
        ssq, rq = sm(NT * H), sm(NT * H)
        sso, ro = sm(NT * H), sm(NT * H)
        bnst = sm(6 * NT)
        mv = sm(2 * NT)
        rv = sm(NT)

        def th(a):
            return a.rearrange("p (t h) -> p t h", t=NT)

        bank = [ctx.enter_context(nc.psum_tensor(f"bank{i}", [P, 512], f32)) for i in range(8)]

        def bank4(b):
            return bank[b][:, :].rearrange("p (h d) -> p h d", h=4)

        X0, X1, Y0, Y1 = 4, 5, 6, 7

        x2 = arena[:, 2:4, 0:D]
        xm = arena[:, 4:6, 0:D]
        xmT = arena[:, 7:9, 0:D].rearrange("p a (k t) -> p a k t", k=HK)
        xgT = blk(6).rearrange("p (k s) -> p k s", k=KC)
        gate_t = blk(7)[:, 0:FE]
        hid = blk(7)[:, FE:2 * FE]
        hidT = blk(8)[:, 0:FE].rearrange("p (j s) -> p j s", j=FC)
        y_sb = blk(9)
        moe_w = arena[:, 13, 0:D]
        fin_w = arena[:, 11, 0:D]
        w_rt = blk(12)[:, 0:KC * (NG + NE)].rearrange("p (k e) -> p k e", k=KC)
        tabs = blk(10)[:, 0:4 * NT * NE].rearrange("p (n t e) -> p n t e", n=4, t=NT)
        assigned, weight, slot, tmp64 = tabs[:, 0], tabs[:, 1], tabs[:, 2], tabs[:, 3]
        onehot = blk(14)[:, 0:NT * P].rearrange("p (t e s) -> p t e s", t=NT, e=EB)
        onehot_w = blk(14)[:, NT * P:2 * NT * P].rearrange("p (t e s) -> p t e s", t=NT, e=EB)
        scatter = blk(15)[:, 0:NT * P]
        lg = blk(15)[:, 512:512 + NT * (NG + NE)].rearrange("p (t e) -> p t e", t=NT)
        zeros = sb("zeros", [P, P])
        upper_strict = sb("upper_strict", [P, P])
        iota_s = sb("iota_s", [P, SL])
        npass_f = sb("npass_f", [P, 8])
        npass_i = sb("npass_i", [P, 2], mybir.dt.int32)
        acc = [[bank[2 * t + n] for n in range(2)] for t in range(NT)]
        y_out = arena[:, 16:18, 0:D]
        r8 = sb("r8", [P, 16, 8])
        r8i = sb("r8i", [P, 2, 8], u32)
        r8e = sb("r8e", [P, 8])

        block = ctx.enter_context(nc.Block())

        @block.sync
        def _(sp):
            for t in range(NT):
                sp.dma_start(x_sb[:, t, :], x[0, t * P:(t + 1) * P, :]).then_inc(S[f"x_loaded{t}"], 16)
            for m, (kind, c) in enumerate(FRONT):
                slot_m = ring[:, m % R, :]
                if m >= R:
                    sp.wait_ge(*S.at("proj_done", units_through(m - R)))
                if kind == "in":
                    src = w_in[0, :, c:c + BW].rearrange("(p k) n -> p k n", k=KC)
                    dst = slot_m.rearrange("p (k n) -> p k n", k=KC)
                elif kind == "branch":
                    src = w_branch[0, c].rearrange("(k p) n -> p k n", p=P)
                    dst = slot_m.rearrange("p (k n) -> p k n", k=NCH)
                else:
                    src = w_out[0, :, c:c + BW].rearrange("(k p) n -> p k n", p=P)
                    dst = slot_m.rearrange("p (k n) -> p k n", k=KC)
                sp.dma_start(dst, src).then_inc(S[f"ring_full{m % R}"], 16)

            def batch(it, b, first=False):
                for j in range(PB):
                    m = NF + j
                    dst = ring[:, m % R, :]
                    if j < 2 * HK:
                        w = w_up if j % 2 else w_gate
                        kp = j // 2
                        src = w[0, bass.ds(b * EB, EB)].rearrange(
                            "e (p k) n -> p e k n", k=KC)[:, :, 2 * kp:2 * kp + 2, :]
                        dst = dst.rearrange("p (e k n) -> p e k n", e=EB, k=2)
                    else:
                        src = w_down[0, bass.ds(b * EB, EB)].rearrange(
                            "e (p j) n -> p e j n", j=FC)[:, :, j - 2 * HK, :]
                        dst = dst.rearrange("p (e n) -> p e n", e=EB)
                    if first and j < R:
                        sp.wait_ge(*S.at("proj_done", units_through(m - R)))
                    else:
                        sp.wait_ge(*S.at("ring_free", it * PB + (j - R + 1)))
                    sp.dma_start(dst, src).then_inc(S[f"ring_full{m % R}"], 16)

            batch(0, 0, first=True)
            with sp.Fori(1, NB) as b:
                batch(b, b)
            sp.wait_ge(*S.at("npass_ready", 1))
            n = sp.value_load(npass_i[0:1, 0:1], min_val=1, max_val=SEQ // SL)
            with sp.If(n > 1):
                with sp.Fori(1, n) as ps:
                    with sp.Fori(0, NB) as b:
                        batch(ps * NB + b, b)

        @block.gpsimd
        def _(pool):
            made = [0]

            def put(ins):
                made[0] += 1
                ins.then_inc(S["pool_chain"], 1)
                pool.wait_ge(*S.at("pool_chain", made[0]))

            def keep(t, pattern, base, cm, op=ALU.is_ge, fill=0.0):
                put(nc.gpsimd.affine_select(out=t, in_=t, compare_op=op, fill=fill, base=base,
                                            pattern=pattern, channel_multiplier=cm))

            NCK = P // CH

            def in_chunk(t):
                v = t.rearrange("p (b c) -> p b c", c=CH)
                keep(v, [[-CH, NCK], [0, CH]], 0, 1)
                keep(v, [[CH, NCK], [0, CH]], CH - 1, -1)

            put(nc.gpsimd.memset(ident[:, :], 0.0))
            keep(ident[:, :], [[-1, P]], 0, 1, ALU.not_equal, 1.0)
            nc.gpsimd.memset(ones[:, :], 1.0).then_inc(S["ident_ready"], 1)
            nc.gpsimd.memset(mhalf, -0.5)
            put(nc.gpsimd.memset(same_chunk[:, :], 1.0))
            in_chunk(same_chunk[:, :])
            pool.wait_ge(*S.at("ss_ready", 1))
            nc.gpsimd.tensor_tensor(rs, ss, mhalf[:, 0:NT], ALU.pow).then_inc(S["rs_ready"], 1)
            for t in (k_in, q_in, v_in):
                nc.gpsimd.memset(t[:, :, 0:TAPS - 1], 0.0)
            put(nc.gpsimd.memset(conf_pad[:, :, 0:CTAPS - 1], 0.0))
            for t, sign, strict in ((up_incl, 1, 0), (lo_incl, -1, 0), (lo_strict, -1, 1)):
                put(nc.gpsimd.tensor_copy(t[:, :], same_chunk[:, :]))
                keep(t[:, :], [[sign, P]], -strict, -sign)
            pool.sem_inc(S["pads_ready"], 1)
            put(nc.gpsimd.memset(merge[:, :, :], 0.0))
            put(nc.gpsimd.memset(merge_lo[:, :], 0.0))
            for n in range(NM):
                s = 1 << n
                v = merge[:, n, :].rearrange("p (b h c) -> p b h c", h=2, c=s)[:, :, 1, :]
                put(nc.gpsimd.memset(v, 1.0))
                keep(v, [[-2 * s, P // (2 * s)], [0, s]], 0, 1)
                keep(v, [[2 * s, P // (2 * s)], [0, s]], s - 1, -1)
            keep(merge_lo[:, :].rearrange("p (b h) -> p b h", h=2)[:, :, 0], [[-2, P // 2]], -1, 1,
                 ALU.not_equal, 1.0)
            put(nc.gpsimd.memset(upper_strict[:, :], 1.0))
            keep(upper_strict[:, :], [[1, P]], -1, -1)
            put(nc.gpsimd.iota(iota_s[:, :], pattern=[[1, SL]], base=0, channel_multiplier=0,
                               allow_small_or_imprecise_dtypes=True))
            pool.sem_inc(S["masks_ready"], 1)
            pool.wait_ge(*S.at("ws_taken", 1))
            nc.gpsimd.affine_select(out=wcT[:, :, :], in_=wcT[:, :, :], compare_op=ALU.is_ge, fill=0.0, base=0,
                                    pattern=[[0, H], [1, P]], channel_multiplier=-1).then_inc(S["wc_ready"], 1)
            for name, dst, src in (("k", rk, ssk), ("q", rq, ssq)):
                pool.wait_ge(*S.at(f"ss{name}_ready", 1))
                nc.gpsimd.tensor_tensor(dst, src, mhalf[:, 0:NT * H], ALU.pow).then_inc(S[f"r{name}_ready"], 1)
            pool.wait_ge(*S.at("gm_var", 1))
            nc.gpsimd.tensor_tensor(rv, rv, mhalf[:, 0:NT], ALU.pow).then_inc(S["gm_rstd"], 1)
            pool.wait_ge(*S.at("sso_ready", 1))
            nc.gpsimd.tensor_tensor(ro, sso, mhalf[:, 0:NT * H], ALU.pow).then_inc(S["ro_ready"], 1)
            pool.wait_ge(*S.at("cf_var", 1))
            nc.gpsimd.tensor_tensor(rv, rv, mhalf[:, 0:NT], ALU.pow).then_inc(S["cf_rstd"], 1)
            for t in range(NT):
                pool.wait_ge(*S.at("ss2_ready", t + 1))
                nc.gpsimd.tensor_tensor(rs[:, t:t + 1], ss[:, t:t + 1], mhalf[:, 0:1],
                                        ALU.pow).then_inc(S["rs2_ready"], 1)
            pool.wait_ge(*S.at("ss3_ready", 1))
            nc.gpsimd.tensor_tensor(rs, ss, mhalf[:, 0:NT], ALU.pow).then_inc(S["rs3_ready"], 1)

        @block.tensor
        def _(pe):
            mm = nc.tensor.matmul

            def unit(m, h):
                u = UNIT[m, h]
                kind, c0 = FRONT[m]
                dst = bank[u % 4]
                if h == 0:
                    pe.wait_ge(*S.at(f"ring_full{m % R}", 16 * (m // R + 1)))
                if u >= 4:
                    name, count = bank_free(u - 4)
                    pe.wait_ge(*S.at(name, count))
                nk = NCH if kind == "branch" else KC
                w = ring[:, m % R, :].rearrange("p (k n) -> p k n", k=nk)
                if m in TOKEN_MAJOR:
                    for k in range(nk):
                        x_t = (xnT[:, k, h * P:(h + 1) * P] if kind == "in" else
                               merged[:, k // NCH, k % NCH, h * P:(h + 1) * P])
                        last = mm(dst[:, :], x_t, w[:, k, :], start=k == 0, stop=k == nk - 1)
                else:
                    src = {3: workA, 2: workB, 1: conf_acc, 0: workA}[c0] if kind == "branch" else xnT
                    for c in range(2):
                        o = (2 * h + c) * P
                        for k in range(nk):
                            last = mm(dst[:, c * SEQ:(c + 1) * SEQ], w[:, k, o:o + P], src[:, k, :],
                                      start=k == 0, stop=k == nk - 1)
                last.then_inc(S["proj_done"], 1)

            def tr(dst, src, n=P):
                return nc.tensor.transpose(dst, src, ident[0:n, 0:n])

            pe.wait_ge(*S.at("ident_ready", 1))
            pe.wait_ge(*S.at("xn_ready", NT))
            for k in range(KC):
                for t in range(NT):
                    last = tr(bank[k // 2][:, (k % 2) * SEQ + t * P:(k % 2) * SEQ + (t + 1) * P], xn[:, t, k::KC])
                if k % 2:
                    last.then_inc(S["xT_done"], 1)
            pe.wait_ge(*S.at("prm_loaded", 16 * 8))
            for c in range(NCH):
                last = tr(bank[X0][:, c * 52:c * 52 + NPRM], prm_rows[:, c * P:(c + 1) * P], NPRM)
            last.then_inc(S["prm_done"], 1)
            pe.wait_ge(*S.at("ws_loaded", 16))
            for g in range(H):
                last = tr(bank4(X1)[:, g, :], ws_sb[:, g, :])
            last.then_inc(S["ws_done"], 1)
            pe.wait_ge(*S.at("xnT_dve", 2))
            pe.wait_ge(*S.at("xnT_act", 2))
            pe.wait_ge(*S.at("wab_loaded", 16))
            for t in range(NT):
                for k in range(KC):
                    last = mm(bank[Y0][:, t * 2 * H:(t + 1) * 2 * H], xnT[:, k, t * P:(t + 1) * P],
                              w_abs[:, k, :], start=k == 0, stop=k == KC - 1)
            last.then_inc(S["ab_done"], 1)

            def decays():
                pe.wait_ge(*S.at("g_ready", 1))
                pe.wait_ge(*S.at("pads_ready", 1))
                for t in range(NT):
                    g_t = th(gl)[:, t, :]
                    mm(bank[Y1][:, t * 2 * H:t * 2 * H + H], up_incl[:, :], g_t, start=True, stop=True)
                    last = mm(bank[Y1][:, t * 2 * H + H:(t + 1) * 2 * H], same_chunk[:, :], g_t,
                              start=True, stop=True)
                last.then_inc(S["gc_done"], 1)
                pe.wait_ge(*S.at("prm_taken", 1))
                pe.wait_ge(*S.at("ws_taken", 1))
                for t in range(NT):
                    for h in range(H):
                        last = mm(bank4(X0 + t)[:, h, :], g_wide[:, t, h, :], up_incl[:, :], start=True, stop=True)
                last.then_inc(S["rows_done"], 1)

            COUNTS = {"kn_ready": NT, "qn_ready": NT, "vb_ready": NT, "decay_taken": NT, "KK_taken": NT * H}

            def transposes(ready, taken, done, dst0, src):
                pe.wait_ge(*S.at(ready, COUNTS.get(ready, 1)))
                for name in taken:
                    pe.wait_ge(*S.at(name, COUNTS.get(name, 1)))
                for t in range(NT):
                    for h in range(H):
                        last = tr(bank4(dst0 + t)[:, h, :], src(t, h))
                last.then_inc(S[done], 1)

            def products(waits, done, dst0, lhsT, rhs):
                for name, n in waits:
                    pe.wait_ge(*S.at(name, n))
                for t in range(NT):
                    for h in range(H):
                        last = mm(bank4(dst0 + t)[:, h, :], lhsT[:, t, h, :], rhs[:, t, h, :], start=True, stop=True)
                last.then_inc(S[done], 1)

            def merge_u(n):
                products([("QM_ready", n), ("T_ready", n), ("LT_taken" if n == 1 else "W_taken", 1 if n == 1 else n - 1)],
                         "U_done", Y0, QM, T_)

            def merge_w(n):
                waits = [("U_taken", n), ("AT_taken" if n == 1 else "W_taken", 1 if n == 1 else n - 1)]
                if n < NM - 1:
                    products(waits, "TU_done", X0, V_, U_)
                products(waits, "TUt_done", Y0, U_, V_)

            def solve():
                products([("vb_ready", NT), ("W_taken", NM - 1)], "u_done", X0, V_, vb_tok)
                products([("kbg_ready", 1)], "wT_done", Y0, kbg_tok, V_)

            def chunk_v(c):
                t, b = divmod(c, P // CH)
                r = slice(b * CH, (b + 1) * CH)
                pe.wait_ge(*S.at("wT_taken", 1))
                pe.wait_ge(*S.at("u_taken", 1))
                pe.wait_ge(*S.at("state_ready", c))
                pe.wait_ge(*S.at("mix_taken", NCH))
                for h in range(H):
                    last = mm(bank4(X0 + t)[r, h, :], wT[:, t, h, r], state[:, h, :], start=True, stop=True)
                last.then_inc(S["ws_state"], 1)

            def chunk_o(c):
                t, b = divmod(c, P // CH)
                r = slice(b * CH, (b + 1) * CH)
                pe.wait_ge(*S.at("vn_ready", c + 1))
                pe.wait_ge(*S.at("wT_taken", 1))
                pe.wait_ge(*S.at("kd_ready", 1))
                if c:
                    pe.wait_ge(*S.at("o_taken", c))
                    pe.wait_ge(*S.at("state_ready", c))
                for h in range(H):
                    if c:
                        mm(bank4(Y0)[r, h, :], qdT[:, t, h, r], state[:, h, :], start=True, stop=False)
                    last = mm(bank4(Y0)[r, h, :], AT[r, t, h, r], vn_tok[r, t, h, :], start=c == 0, stop=True)
                last.then_inc(S["o_done"], 1)
                if c < 3:
                    for h in range(H):
                        last = mm(bank4(Y1)[:, h, :], k_tok[r, t, h, :], vn_tok[r, t, h, :], start=True, stop=True)
                    last.then_inc(S["state_add"], 1)

            def mixed():
                pe.wait_ge(*S.at("gm_ln", 1))
                pe.wait_ge(*S.at("wc_ready", 1))
                pe.wait_ge(*S.at("u_taken", 1))
                for g in range(H):
                    for t in range(NT):
                        o = (g % 2) * SEQ + t * P
                        last = mm(bank[X0 + g // 2][:, o:o + P], gm_v[:, t, g * P:(g + 1) * P], wcT[:, g, :],
                                  start=True, stop=True)
                last.then_inc(S["mix_done"], 1)

            def conf_fwd():
                pe.wait_ge(*S.at("cf_conv", NCH))
                pe.wait_ge(*S.at("o_taken", 4))
                pe.wait_ge(*S.at("state_ready", 3))
                for t in range(NT):
                    for c in range(NCH):
                        last = tr(bank4(Y0 + t)[:, c, :], conf_acc[:, c, t * P:(t + 1) * P])
                last.then_inc(S["cfT_done"], 1)

            def conf_back():
                pe.wait_ge(*S.at("cf_norm", NT))
                for c in range(NCH):
                    for t in range(NT):
                        last = tr(bank[Y0 + c // 2][:, (c % 2) * SEQ + t * P:(c % 2) * SEQ + (t + 1) * P],
                                  cf_tok[:, t, c, :])
                last.then_inc(S["cfB_done"], 1)

            def o_back():
                pe.wait_ge(*S.at("on_ready", 1))
                for h in range(H):
                    for t in range(NT):
                        last = tr(bank[X0 + h // 2][:, (h % 2) * SEQ + t * P:(h % 2) * SEQ + (t + 1) * P],
                                  o_tok[:, t, h, :])
                last.then_inc(S["oT_done"], 1)

            after = {
                (PK, 1): [decays],
                (PQ, 1): [lambda: transposes("k_act", ("ab_taken", "gc_taken", "egc_ready"), "kf_done", Y0, lambda t, h: k_ch[:, h, t * P:(t + 1) * P])],
                (PV, 1): [lambda: transposes("q_act", ("decay_taken", "egl_ready"), "qf_done", X0, lambda t, h: q_ch[:, h, t * P:(t + 1) * P])],
                (PCA, 0): [lambda: transposes("kn_ready", ("sqk_done",), "kb_done", Y0, lambda t, h: k_tok[:, t, h, :])],
                (PCA, 1): [lambda: transposes("v_act", ("qn_ready",), "vf_done", X0, lambda t, h: v_ch[:, h, t * P:(t + 1) * P])],
                (PCG, 0): [lambda: products([("kT_ready", 1)], "KK_done", Y0, kT, kT)],
                (PCG, 1): [lambda: transposes("qn_ready", ("vb_ready",), "qb_done", X0, lambda t, h: q_tok[:, t, h, :])],
                (PSC, 0): [lambda: transposes("qd_ready", ("KK_taken",), "qdb_done", Y0, lambda t, h: qd_tok[:, t, h, :])],
                (PSC, 1): [lambda: products([("qT_ready", 1)], "QK_done", X0, qT, kT)],
                (PSX, 0): [lambda: transposes("L_ready", ("qdT_ready",), "LT_done", Y0, lambda t, h: L_[:, t, h, :])],
                (PSX, 1): [lambda: transposes("A_ready", (), "AT_done", X0, lambda t, h: A_[:, t, h, :])],
                (PSB, 0): [lambda: merge_u(1)], (PSB, 1): [lambda: merge_w(1)],
                (PG3A, 0): [lambda: merge_u(2)], (PG3A, 1): [lambda: merge_w(2)],
                (PG3B, 0): [lambda: merge_u(3)], (PG3B, 1): [lambda: merge_w(3)],
                (PW3, 1): [lambda: merge_u(4)], (PW3, 3): [lambda: merge_w(4)],
                (PGV, 0): [lambda: merge_u(5)], (PGV, 1): [lambda: merge_w(5)],
                (PGU, 1): [solve],
                (PG2A, 0): [lambda: chunk_o(0), mixed],
                (PG2A, 1): [lambda: chunk_v(1)],
                (PG2B, 0): [lambda: chunk_o(1)],
                (PW2, 0): [lambda: chunk_v(2)],
                (PW2, 3): [lambda: chunk_o(2)],
                (PZ, 0): [lambda: chunk_v(3)],
                (PZ, 1): [lambda: chunk_o(3)],
                (PG1A, 0): [conf_fwd],
                (PG1A, 1): [o_back],
                (PG1B, 0): [conf_back],
            }
            for u, key in enumerate(UNITS):
                if key == (PW3, 0):
                    pe.wait_ge(*S.at("proj_taken_dve", bank_free(UNIT[PSB, 1])[1]))
                if key == (PW2, 0):
                    pe.wait_ge(*S.at("y2_ready", 1))
                if key == (PW1, 0):
                    pe.wait_ge(*S.at("y1_ready", 1))
                if key == (PW0, 0):
                    pe.wait_ge(*S.at("y0_ready", 1))
                if key == (PO0, 0):
                    pe.wait_ge(*S.at("gate_used", 12))
                unit(*key)
                for step in after.get(key, []):
                    step()

            pe.wait_ge(*S.at("proj_taken_dve", bank_free(len(UNITS) - 1)[1]))
            for t in range(NT):
                for n in range(2):
                    last = mm(acc[t][n][:, :], ident[:, :], x2[:, t, n * BW:(n + 1) * BW], start=True, stop=False)
            for t in range(NT):
                pe.wait_ge(*S.at("xm_ready", t + 1))
                for k in range(KC):
                    last = tr(bank4(X0 + 2 * t + k // HK)[:, k % HK, :], xm[:, t, k * P:(k + 1) * P])
                last.then_inc(S["xmT_done"], 1)
            pe.wait_ge(*S.at("rt_loaded", 16 * 2))
            for t in range(NT):
                pe.wait_ge(*S.at("xmT_act", t + 1))
                pe.wait_ge(*S.at("xmT_dve", t + 1))
                for k in range(KC):
                    last = mm(bank[X0 + t][:, 0:NG + NE], xmT[:, k // HK, k % HK, t * P:(t + 1) * P],
                              w_rt[:, k, :], start=k == 0, stop=k == KC - 1)
                last.then_inc(S["logits_done"], 1)
            pe.wait_ge(*S.at("assigned_ready", 1))
            for t in range(NT):
                for s in range(t):
                    mm(bank[Y0][:, t * NE:(t + 1) * NE], ones[:, :], assigned[:, s, :], start=s == 0, stop=False)
                last = mm(bank[Y0][:, t * NE:(t + 1) * NE], upper_strict[:, :], assigned[:, t, :],
                          start=t == 0, stop=True)
            for t in range(NT):
                last = mm(bank[Y1][:, 0:NE], ones[:, :], assigned[:, t, :], start=t == 0, stop=t == NT - 1)
            last.then_inc(S["counts_done"], 1)

            pe.wait_ge(*S.at("npass_ready", 1))
            pe.sem_inc(S["xg_done"], 1)
            pe.sem_inc(S["scatter_done"], 1)
            pe.sem_inc(S["summed"], 1)
            n = pe.value_load(npass_i[0:1, 0:1], min_val=1, max_val=SEQ // SL)
            with pe.Fori(0, n) as ps:
                with pe.Fori(0, NB) as b:
                    it = ps * NB + b
                    pe.wait_ge(*S.at("onehot_ready", it + 1))
                    pe.wait_ge(*S.at("y_taken_act", it + 1))
                    pe.wait_ge(*S.at("y_taken_dve", it + 1))
                    for k in range(KC):
                        for t in range(NT):
                            last = mm(bank4(Y0 + k // HK)[:, k % HK, :], xm[:, t, k * P:(k + 1) * P],
                                      onehot[:, t].rearrange("p e s -> p (e s)"), start=t == 0, stop=t == NT - 1)
                        if k % HK == HK - 1:
                            last.then_inc(S["xg_done"], 1)
                    pe.wait_ge(*S.at("hidT_taken", it + 1))
                    pe.wait_ge(*S.at("onehot_w_ready", it + 1))
                    for t in range(NT):
                        last = tr(bank[X0][:, t * P:(t + 1) * P], onehot_w[:, t].rearrange("p e s -> p (e s)"))
                    last.then_inc(S["scatter_done"], 1)
                    pe.wait_ge(*S.at("scatter_taken", it + 1))
                    for j in range(2 * HK):
                        m = NF + j
                        w = ring[:, m % R, :].rearrange("p (e k n) -> p e k n", e=EB, k=2)
                        dst = bank[X1] if j % 2 else bank[X0]
                        if j == 0:
                            pe.wait_ge(*S.at("xg_taken_act", it + 1))
                            pe.wait_ge(*S.at("xg_taken_dve", it + 1))
                        pe.wait_ge(*S.at(f"ring_full{m % R}", it * (16 * PB // R) + 16 * (m // R + 1)))
                        for kk in range(2):
                            k = 2 * (j // 2) + kk
                            for e in range(EB):
                                rows = slice(e * SL, (e + 1) * SL)
                                last = mm(dst[rows, :], xgT[:, k, rows], w[:, e, kk, :],
                                          start=k == 0, stop=k == KC - 1)
                        last.then_inc(S["ring_free"], 1)
                    pe.wait_ge(*S.at("hid_ready", it + 1))
                    for j in range(FC):
                        last = tr(bank4(X0)[:, j, :], hid[:, j::FC])
                    last.then_inc(S["hidT_done"], 1)
                    pe.wait_ge(*S.at("hidT_taken", it + 2))
                    for j in range(FC):
                        m = NF + 2 * HK + j
                        w = ring[:, m % R, :].rearrange("p (e n) -> p e n", e=EB)
                        pe.wait_ge(*S.at(f"ring_full{m % R}", it * (16 * PB // R) + 16 * (m // R + 1)))
                        for n2 in range(2):
                            for e in range(EB):
                                rows = slice(e * SL, (e + 1) * SL)
                                last = mm(bank[Y0 + n2][rows, :], hidT[:, j, rows],
                                          w[:, e, n2 * BW:(n2 + 1) * BW], start=j == 0, stop=j == FC - 1)
                        last.then_inc(S["ring_free"], 1)
                    pe.wait_ge(*S.at("y_taken_act", it + 2))
                    pe.wait_ge(*S.at("y_taken_dve", it + 2))
                    for t in range(NT):
                        for n2 in range(2):
                            last = mm(acc[t][n2][:, :], scatter[:, t * P:(t + 1) * P],
                                      y_sb[:, n2 * BW:(n2 + 1) * BW], start=False, stop=False)
                    last.then_inc(S["summed"], 1)
            for t in range(NT):
                for n2 in range(2):
                    last = mm(acc[t][n2][:, :], zeros[:, :], y_sb[:, n2 * BW:(n2 + 1) * BW],
                              start=False, stop=True)
            last.then_inc(S["sum_closed"], 1)

        @block.vector
        def _(dve):
            V = nc.vector
            made = [0]

            def do(ins):
                made[0] += 1
                ins.then_inc(S["dve_chain"], 1)
                return made[0]

            def need(n):
                dve.wait_ge(*S.at("dve_chain", n))

            def link(ins):
                need(do(ins))

            def tell(ins, name):
                ins.then_inc(S[name], 1)

            def wait(name, n=1):
                dve.wait_ge(*S.at(name, n))

            def wide(v, n):
                return v.unsqueeze(2).to_broadcast([P, v.shape[1], n])

            def rows(m, n):
                return m.unsqueeze(1).to_broadcast([P, n, m.shape[-1]])

            def conv(src, dst, row, taps, name=None, chunks=range(NCH), first=0, last=None):
                last = taps if last is None else last
                at = {}
                for j in range(first, last):
                    for c in chunks:
                        x_j = src[:, c, j:j + SEQ]
                        w_j = prm[:, c, row + j:row + j + 1]
                        if c in at:
                            need(at[c])
                        if j == 0:
                            ins = V.tensor_scalar(dst[:, c, :], x_j, w_j, None, ALU.mult)
                        else:
                            ins = V.scalar_tensor_tensor(dst[:, c, :], x_j, w_j, dst[:, c, :], ALU.mult, ALU.add)
                        if name and j == last - 1 and c == chunks[-1]:
                            tell(ins, name)
                            wait(name)
                        else:
                            at[c] = do(ins)
                need(made[0])

            link(V.memset(zeros[:, :], 0.0))
            wait("sq_done", NT)
            tell(V.tensor_scalar(ss, ss, 1.0 / D, EPS, ALU.mult, ALU.add), "ss_ready")
            wait("rs_ready")
            for t in range(NT):
                tell(V.tensor_scalar(xn[:, t, :], x_sb[:, t, :], rs[:, t:t + 1], None, ALU.mult), "xn_ready")
            wait("mix_loaded", 16)
            for b in range(2):
                wait("xT_done", b + 1)
                tell(V.tensor_tensor(xnT[:, 2 * b:2 * b + 2, :], bank[b][:, :].rearrange("p (k t) -> p k t", k=2),
                                     wide(w_mix[:, 2 * b:2 * b + 2], SEQ), ALU.mult), "xnT_dve")
            wait("prm_done")
            tell(V.tensor_copy(prm[:, :, 0:NPRM],
                               bank[X0][:, 0:NCH * 52].rearrange("p (c r) -> p c r", c=NCH)[:, :, 0:NPRM]), "prm_taken")
            wait("ws_done")
            tell(V.tensor_copy(wcT[:, :, :], bank4(X1)), "ws_taken")
            wait("prm_taken")
            link(V.tensor_scalar(prm[:, :, RLW:RLB + 1], prm[:, :, RLW:RLB + 1], 0.5, None, ALU.mult))

            wait("ab_done")
            wait("small_loaded", 48)
            ab = bank[Y0][:, 0:NT * 2 * H].rearrange("p (t c) -> p t c", t=NT)
            wait("beta_tanh")
            link(V.tensor_tensor(th(e1), ab[:, :, H:2 * H], rows(dtb, NT), ALU.add))
            tell(V.scalar_tensor_tensor(e2, e1, -1.0, e1, ALU.mult, ALU.max), "abs_ready")
            link(V.tensor_scalar(beta, beta, 0.5, 0.5, ALU.mult, ALU.add))
            tell(V.tensor_scalar(e1, e1, 0.0, None, ALU.max), "ab_taken")
            wait("log_ready")
            wait("ab_taken")
            link(V.tensor_tensor(e1, e1, e3, ALU.add))
            link(V.tensor_tensor(th(e1), th(e1), rows(expA, NT), ALU.mult))
            link(V.tensor_scalar(gl, e1, -1.0, None, ALU.mult))
            wait("xT_done", 4)
            tell(V.tensor_copy(g_wide, gl.rearrange("p (t h) -> p t h", t=NT).unsqueeze(3).to_broadcast([P, NT, H, P])),
                 "g_ready")

            def silu(ch, t2, name):
                wait(name + "_tanh")
                tell(V.scalar_tensor_tensor(ch, t2, 1.0, ch, ALU.add, ALU.mult), name + "_act")

            wait("pads_ready")
            wait("proj_taken_act", 2)
            conv(k_in, k_ch, RK, TAPS, "k_conv")

            wait("gc_done")
            gc = bank[Y1][:, 0:NT * 2 * H].rearrange("p (t c) -> p t c", t=NT)
            link(V.tensor_copy(th(gcum), gc[:, :, 0:H]))
            tell(V.tensor_tensor(th(e2), gc[:, :, H:2 * H], th(gcum), ALU.subtract), "gc_taken")
            wait("rows_done")
            for t in range(NT):
                tell(V.tensor_tensor(decay[:, t], bank4(X0 + t), wide(th(gcum)[:, t, :], P), ALU.subtract), "decay_taken")
            wait("decay_taken", NT)
            tell(V.tensor_tensor(thf(10), thf(10), rows(lo_incl[:, :], NT * H), ALU.mult), "decay_log")
            wait("egc_ready")
            link(V.tensor_tensor(bgk, beta, egc, ALU.mult))
            silu(k_ch, tan[0], "k")

            wait("proj_taken_act", 4)
            conv(q_in, q_ch, RQ, TAPS, "q_conv")

            def norm(name, ssx):
                wait(f"sq{name}_done")
                link(V.tensor_reduce(ssx, squares, AXX, ALU.add))
                tell(V.tensor_scalar(ssx, ssx, 0.25, EPS, ALU.mult, ALU.add), f"ss{name}_ready")

            wait("sqk_done")
            norm("k", ssk)
            silu(q_ch, tan[1], "q")
            wait("rk_ready")
            link(V.tensor_scalar(rk, rk, 0.5, None, ALU.mult))
            for t in range(NT):
                tell(V.tensor_tensor(k_tok[:, t], bank4(Y0 + t), wide(th(rk)[:, t, :], P), ALU.mult), "kn_ready")
            wait("kn_ready", NT)
            tell(V.tensor_tensor(thf(1), thf(0), wide(bgk, P), ALU.mult), "kbg_ready")

            wait("proj_taken_act", 6)
            conv(v_in, v_ch, RV, TAPS, "v_conv")
            norm("q", ssq)
            wait("rq_ready")
            link(V.tensor_scalar(rq, rq, 0.5 * float(P) ** -0.5, None, ALU.mult))
            for t in range(NT):
                tell(V.tensor_tensor(q_tok[:, t], bank4(X0 + t), wide(th(rq)[:, t, :], P), ALU.mult), "qn_ready")
            wait("qn_ready", NT)
            silu(v_ch, tan[0], "v")
            tell(V.tensor_tensor(thf(3), thf(2), wide(egc, P), ALU.mult), "qd_ready")
            link(V.tensor_scalar(e1, beta, 0.5, None, ALU.mult))
            wait("vf_done")
            for t in range(NT):
                tell(V.tensor_tensor(vb_tok[:, t], bank4(X0 + t), wide(th(e1)[:, t, :], P), ALU.mult), "vb_ready")
            wait("kb_done")
            wait("ekd_ready")
            tell(V.tensor_tensor(thf(0), thf(0), wide(ekd, P), ALU.mult), "kd_ready")

            for h in range(2):
                wait("proj_taken_act", bank_free(UNIT[PCG, h])[1])
                a = conf_acc[:, 2 * h:2 * h + 2, :]
                tell(V.scalar_tensor_tensor(conf_pad[:, 2 * h:2 * h + 2, CTAPS - 1:], tan[1][:, 2 * h:2 * h + 2, :], 1.0,
                                            a, ALU.add, ALU.mult), "conf_in")
            conf_parts = [(c0, j) for c0 in (0, 2) for j in range(0, CTAPS, 8)]

            def conf_part():
                if conf_parts:
                    c0, j = conf_parts.pop(0)
                    conv(conf_pad, conf_acc, RC, CTAPS, None, range(c0, c0 + 2), j, min(j + 8, CTAPS))

            wait("conf_in", 2)

            wait("KK_done")
            wait("decay_exp")
            for t in range(NT):
                for h in range(H):
                    tell(V.scalar_tensor_tensor(L_[:, t, h], bank4(Y0 + t)[:, h, :], th(beta)[:, t, h:h + 1],
                                                decay[:, t, h], ALU.mult, ALU.mult), "KK_taken")
            wait("KK_taken", NT * H)
            tell(V.tensor_tensor(thf(11), thf(11), rows(lo_strict[:, :], NT * H), ALU.mult), "L_ready")
            conf_part()
            wait("QK_done")
            for t in range(NT):
                ins = V.tensor_tensor(A_[:, t], bank4(X0 + t), decay[:, t], ALU.mult)
                link(ins) if t == 0 else tell(ins, "A_masked")
            wait("A_masked")
            tell(V.tensor_tensor(thf(13), thf(13), rows(lo_incl[:, :], NT * H), ALU.mult), "A_ready")

            for h in range(2):
                u = UNIT[PSX, h]
                wait("proj_done", u + 1)
                wait("proj_taken_act", bank_free(UNIT[PSC, h])[1])
                tell(V.tensor_tensor(cx[:, 2 * h:2 * h + 2, STAPS - 1:], workA[:, 2 * h:2 * h + 2, :],
                                     bank[u % 4][:, :].rearrange("p (c t) -> p c t", c=2), ALU.mult), "proj_taken_dve")
            link(V.memset(cx[:, :, 0:STAPS - 1], 0.0))
            wait("proj_taken_dve", 2)
            conv(cx, workA, RS, STAPS)

            wait("LT_taken")
            wait("qdT_ready")
            link(V.tensor_tensor(thf(3), thf(12), rows(merge[:, 0, :], NT * H), ALU.mult))
            link(V.scalar_tensor_tensor(thf(3), thf(3), -1.0, rows(ident[:, :], NT * H), ALU.mult, ALU.add))
            link(V.tensor_tensor(thf(2), thf(11), rows(merge_lo[:, :], NT * H), ALU.mult))
            tell(V.scalar_tensor_tensor(thf(2), thf(2), -1.0, rows(ident[:, :], NT * H), ALU.mult, ALU.add), "T_ready")

            def merge_mask(n):
                wait("T_ready", 1)
                if n > 1:
                    wait("U_done", n - 1)
                tell(V.tensor_tensor(thf(11), thf(12), rows(merge[:, n, :], NT * H), ALU.mult), "QM_ready")

            def merge_take(n):
                if n < NM - 1:
                    wait("TU_done", n)
                wait("TUt_done", n)
                for t in range(NT):
                    if n < NM - 1:
                        last = V.tensor_tensor(T_[:, t], T_[:, t], bank4(X0 + t), ALU.subtract)
                        tell(last, "T_ready") if t else do(last)
                for t in range(NT):
                    last = V.tensor_tensor(V_[:, t], V_[:, t], bank4(Y0 + t), ALU.subtract)
                    tell(last, "W_taken") if t else do(last)

            def sc_out(h):
                u = UNIT[PSB, h]
                wait("proj_done", u + 1)
                w = workA[:, 2 * h:2 * h + 2, :]
                tell(V.tensor_tensor(w, w, bank[u % 4][:, :].rearrange("p (c t) -> p c t", c=2), ALU.mult),
                     "proj_taken_dve")

            def branch_unit(m, q):
                u = UNIT[m, q]
                c = 2 * (q % 2)
                wait("proj_taken_act", bank_free(UNIT[GATES[m] + q // 2, q % 2])[1])
                wait("proj_done", u + 1)
                g = tan[q // 2][:, c:c + 2, :]
                o = merged[:, q // 2, c:c + 2, :]
                ps = bank[u % 4][:, :].rearrange("p (c t) -> p c t", c=2)
                if m == PW3:
                    tell(V.scalar_tensor_tensor(o, g, 1.0, ps, ALU.add, ALU.mult), "proj_taken_dve")
                else:
                    tell(V.scalar_tensor_tensor(g, g, 1.0, ps, ALU.add, ALU.mult), "proj_taken_dve")
                    wait("proj_taken_dve", bank_free(u)[1])
                    tell(V.tensor_tensor(o, o, g, ALU.add), "gate_used")

            GATES = {PW3: PG3A, PW2: PG2A, PW1: PG1A, PW0: PG0A}

            merge_mask(1)
            sc_out(0)
            conf_part()
            sc_out(1)
            conf_part()
            merge_take(1)
            merge_mask(2)
            conf_part()
            merge_take(2)
            merge_mask(3)
            conf_part()
            merge_take(3)
            merge_mask(4)
            for q in range(4):
                branch_unit(PW3, q)
                if q == 1:
                    conf_part()
            merge_take(4)
            merge_mask(5)

            GC = 0.7978845608028654

            def gelu_unit(n, m, h, dst):
                u = UNIT[m, h]
                ps = bank[u % 4][:, :]
                s = blk(16 + n // 2)[:, (n % 2) * 512:(n % 2 + 1) * 512]
                wait("gelu_sq", n + 1)
                link(V.tensor_scalar(s, s, 0.044715, 1.0, ALU.mult, ALU.add))
                tell(V.tensor_tensor(s, s, ps, ALU.mult), "gelu_in")
                yield
                wait("gelu_tanh", n + 1)
                tell(V.scalar_tensor_tensor(dst, s, 1.0, ps, ALU.add, ALU.mult), "proj_taken_dve")

            def layer_stats(src, t):
                link(V.bn_stats(bnst[:, 6 * t:6 * t + 6], src))
                link(V.bn_aggr(mv[:, 2 * t:2 * t + 2], bnst[:, 6 * t:6 * t + 6]))

            for t in range(NT):
                g = gelu_unit(t, PGV, t, gm_v[:, t, :])
                next(g)
                next(g, None)
                wait("proj_taken_dve", bank_free(UNIT[PGV, t])[1])
                layer_stats(gm_v[:, t, :], t)
            merge_take(5)
            mvv = mv.rearrange("p (t c) -> p t c", t=NT)
            tell(V.tensor_scalar(rv, mvv[:, :, 1], 4 * EPS, None, ALU.add), "gm_var")
            conf_part()
            wait("gm_rstd")
            for t in range(NT):
                do(V.tensor_scalar(gm_v[:, t, :], gm_v[:, t, :], mvv[:, t, 0:1], rv[:, t:t + 1],
                                   ALU.subtract, ALU.mult))
            need(made[0])
            wait("lnrows_loaded", 32)
            link(V.tensor_tensor(gm_v, gm_v, rows(ln_rows[:, 0, :], NT), ALU.mult))
            tell(V.tensor_tensor(gm_v, gm_v, rows(ln_rows[:, 1, :], NT), ALU.add), "gm_ln")
            for h in range(2):
                g = gelu_unit(NT + h, PGU, h, gm_u[:, 2 * h:2 * h + 2, :].rearrange("p c t -> p (c t)"))
                next(g)
                next(g, None)
            while conf_parts:
                conf_part()
            for c in range(NCH):
                tell(V.tensor_scalar(conf_acc[:, c, :], conf_acc[:, c, :], 0.5, prm[:, c, RCB:RCB + 1],
                                     ALU.mult, ALU.add), "cf_conv")

            def chunk_new(c):
                t, b = divmod(c, P // CH)
                r = slice(b * CH, (b + 1) * CH)
                if c == 0:
                    wait("u_taken")
                    tell(V.tensor_copy(vn_tok[r, t], u_tok[r, t]), "vn_ready")
                else:
                    wait("ws_state", c)
                    tell(V.tensor_tensor(vn_tok[r, t], u_tok[r, t], bank4(X0 + t)[r], ALU.subtract), "vn_ready")

            def chunk_state(c):
                wait("state_add", c + 1)
                if c == 0:
                    tell(V.tensor_copy(state[:, :, :], bank4(Y1)), "state_ready")
                else:
                    wait("ws_state", c)
                    wait("o_done", c + 1)
                    link(V.tensor_tensor(state[:, :, :], state[:, :, :],
                                         wide(egl.rearrange("p (t h b) -> p t h b", t=NT, h=H)[:, c // 2, :, c % 2], P),
                                         ALU.mult))
                    tell(V.tensor_tensor(state[:, :, :], state[:, :, :], bank4(Y1), ALU.add), "state_ready")

            wait("U_done", NM - 1)
            chunk_new(0)
            chunk_state(0)
            wait("mix_done")
            wait("bs_loaded", 16)
            wait("proj_taken_dve", bank_free(UNIT[PGU, 1])[1])
            for n in range(2):
                v = tan[1].rearrange("p (n g) (t i) -> p n g t i", n=2, t=NT)
                for g in range(2):
                    tell(V.tensor_tensor(v[:, n, g], bank[X0 + n][:, g * SEQ:(g + 1) * SEQ].rearrange("p (t i) -> p t i", t=NT),
                                       rows(bs_row[:, 2 * n + g, :], NT), ALU.add), "mix_taken")
            wait("mix_taken", NCH)
            tell(V.scalar_tensor_tensor(workB, tan[1], 0.5, gm_u, ALU.mult, ALU.mult), "y2_ready")
            chunk_new(1)
            chunk_state(1)
            chunk_new(2)
            for q in range(3):
                branch_unit(PW2, q)
            branch_unit(PW2, 3)
            chunk_state(2)
            chunk_new(3)
            for h in range(2):
                u = UNIT[PZ, h]
                z = zbuf[:, 2 * h:2 * h + 2, :]
                wait("z_tanh", h + 1)
                tell(V.scalar_tensor_tensor(z, z, 1.0, bank[u % 4][:, :].rearrange("p (c t) -> p c t", c=2),
                                            ALU.add, ALU.mult), "proj_taken_dve")
            wait("sqo_done")
            link(V.tensor_reduce(sso, squares, AXX, ALU.add))
            tell(V.tensor_scalar(sso, sso, 1.0 / P, EPS, ALU.mult, ALU.add), "sso_ready")
            wait("cfT_done")
            for t in range(NT):
                layer_stats(bank[Y0 + t][:, :], t)
            tell(V.tensor_scalar(rv, mvv[:, :, 1], EPS, None, ALU.add), "cf_var")
            wait("ro_ready")
            tell(V.tensor_tensor(thf(10), thf(10), wide(ro, P), ALU.mult), "on_ready")
            wait("cf_rstd")
            wait("proj_done", UNIT[PW2, 3] + 1)
            for t in range(NT):
                tell(V.tensor_scalar(cf_tok[:, t].rearrange("p c d -> p (c d)"), bank[Y0 + t][:, :], mvv[:, t, 0:1],
                                     rv[:, t:t + 1], ALU.subtract, ALU.mult), "cf_norm")
            wait("oT_done")
            link(V.tensor_scalar(w_gn, w_gn, 0.5, None, ALU.mult))
            wait("proj_taken_dve", bank_free(UNIT[PZ, 1])[1])
            for n in range(2):
                last = V.scalar_tensor_tensor(workA[:, 2 * n:2 * n + 2, :].rearrange("p c t -> p (c t)"), bank[X0 + n][:, :],
                                              w_gn, zbuf[:, 2 * n:2 * n + 2, :].rearrange("p c t -> p (c t)"),
                                              ALU.mult, ALU.mult)
                tell(last, "y0_ready") if n else do(last)
            wait("cf_tanh", 2)
            tell(V.scalar_tensor_tensor(conf_acc, cf_tok.rearrange("p t h d -> p (t h d)").rearrange("p (c t) -> p c t", c=NCH),
                                        1.0, conf_acc, ALU.add, ALU.mult), "y1_ready")
            for m in (PW1, PW0):
                for q in range(4):
                    branch_unit(m, q)
            wait("xres_loaded", 32)
            for n, m in enumerate((PO0, PO1)):
                for t in range(NT):
                    u = UNIT[m, t]
                    wait("proj_done", u + 1)
                    o = x2[:, t, n * BW:(n + 1) * BW]
                    tell(V.scalar_tensor_tensor(o, bank[u % 4][:, :], 0.5, o, ALU.mult, ALU.add), "proj_taken_dve")

            for t in range(NT):
                wait("sq2_done", t + 1)
                tell(V.tensor_scalar(ss[:, t:t + 1], ss[:, t:t + 1], 1.0 / D, EPS, ALU.mult, ALU.add), "ss2_ready")
            wait("moew_loaded", 16)
            for t in range(NT):
                wait("rs2_ready", t + 1)
                tell(V.scalar_tensor_tensor(xm[:, t, :].rearrange("p (k q) -> p q k", k=KC),
                                            x2[:, t, :].rearrange("p (q k) -> p q k", k=KC), rs[:, t:t + 1],
                                            moe_w.rearrange("p (q k) -> p q k", k=KC), ALU.mult, ALU.mult), "xm_ready")
            for t in range(NT):
                wait("xmT_done", t + 1)
                tell(V.tensor_copy(xmT[:, 1, :, t * P:(t + 1) * P], bank4(X1 + 2 * t)), "xmT_dve")
            wait("masks_ready")
            r = [r8[:, n, :] for n in range(16)]
            for t in range(NT):
                wait("logits_done", t + 1)
                lt = lg[:, t, :]
                link(V.tensor_copy(lt, bank[X0 + t][:, 0:NG + NE]))
                gmax, gidx, ohg, ex = r[0], r[1], r[2], r[3]
                link(V.max(gmax, lt[:, 0:NG]))
                link(V.max_index(r8i[:, 0, :], gmax, lt[:, 0:NG]))
                link(V.tensor_copy(gidx, r8i[:, 0, :]))
                link(V.tensor_scalar(ohg, iota_s[:, 0:8], gidx[:, 0:1], None, ALU.is_equal))
                tell(V.tensor_scalar(r[4][:, 0:1], gmax[:, 0:1], -1.0, None, ALU.mult), "ngmax_ready")
                t64 = tmp64[:, t, :].rearrange("p (g e) -> p g e", g=NG)
                link(V.tensor_tensor(t64, lt[:, NG:].rearrange("p (g e) -> p g e", g=NG), wide(ohg, EG), ALU.mult))
                sel, m8, i8 = r[5], r[6], r[7]
                link(V.tensor_reduce(sel, tmp64[:, t, :].rearrange("p (g e) -> p e g", g=NG), AXX, ALU.add))
                link(V.max(m8, sel))
                link(V.max_index(r8i[:, 1, :], m8, sel))
                link(V.tensor_copy(i8, r8i[:, 1, :]))
                link(V.tensor_scalar(r[8], iota_s[:, 0:8], i8[:, 0:1], None, ALU.is_equal))
                link(V.tensor_scalar(r[9], iota_s[:, 0:8], i8[:, 1:2], None, ALU.is_equal))
                tell(V.tensor_tensor(r[10][:, 0:1], m8[:, 1:2], m8[:, 0:1], ALU.subtract), "gap_ready")
                wait("exps_done", t + 1)
                link(V.tensor_scalar(r[11][:, 0:1], r[10][:, 1:2], 1.0, r[4][:, 1:2], ALU.add, ALU.mult))
                link(V.reciprocal(r[11][:, 1:2], r[11][:, 0:1]))
                link(V.tensor_tensor(r[11][:, 2:3], r[11][:, 1:2], r[10][:, 1:2], ALU.mult))
                link(V.tensor_tensor(r[12], r[8], r[9], ALU.add))
                link(V.tensor_scalar(r[13], r[8], r[11][:, 1:2], None, ALU.mult))
                link(V.scalar_tensor_tensor(r[13], r[9], r[11][:, 2:3], r[13], ALU.mult, ALU.add))
                link(V.tensor_tensor(weight[:, t, :].rearrange("p (g e) -> p g e", g=NG), wide(ohg, EG), rows(r[13], NG), ALU.mult))
                link(V.tensor_tensor(assigned[:, t, :].rearrange("p (g e) -> p g e", g=NG), wide(ohg, EG), rows(r[12], NG), ALU.mult))
            tell(V.memset(r[14], 0.0), "assigned_ready")
            wait("counts_done")
            link(V.scalar_tensor_tensor(slot, bank[Y0][:, 0:NT * NE].rearrange("p (t e) -> p t e", t=NT), 1.0,
                                        assigned, ALU.add, ALU.mult))
            link(V.tensor_scalar(slot, slot, -1.0, None, ALU.add))
            link(V.tensor_reduce(npass_f[:, 0:1], bank[Y1][:, 0:NE], AXX, ALU.max))
            link(V.tensor_scalar(r[15], iota_s[:, 0:8], float(SL), None, ALU.mult))
            link(V.tensor_scalar(r[15], r[15], npass_f[:, 0:1], None, ALU.is_lt))
            link(V.tensor_reduce(npass_f[:, 1:2], r[15], AXX, ALU.add))
            tell(V.tensor_copy(npass_i[:, 0:1], npass_f[:, 1:2]), "npass_ready")

            wait("npass_ready")
            dve.sem_inc(S["y_taken_dve"], 1)
            n = dve.value_load(npass_i[0:1, 0:1], min_val=1, max_val=SEQ // SL)
            with dve.Fori(0, n) as ps:
                with dve.Fori(0, NB) as b:
                    it = ps * NB + b
                    wait("xg_done", it * 2 + 1)
                    e4 = bass.ds(b * EB, EB)
                    sl = slot[:, :, e4].unsqueeze(3).to_broadcast([P, NT, EB, SL])
                    io = iota_s[:, :].unsqueeze(1).unsqueeze(1).to_broadcast([P, NT, EB, SL])
                    V.tensor_tensor(onehot, sl, io, ALU.is_equal).then_inc(S["onehot_ready"], 1)
                    wait("onehot_ready", it + 1)
                    wait("scatter_done", it + 1)
                    V.tensor_tensor(onehot_w, onehot, weight[:, :, e4].unsqueeze(3).to_broadcast([P, NT, EB, SL]),
                                    ALU.mult).then_inc(S["onehot_w_ready"], 1)
                    wait("xg_done", it * 2 + 3)
                    V.tensor_copy(xgT[:, HK:KC, :], bank4(Y1)).then_inc(S["xg_taken_dve"], 1)
                    wait("scatter_done", it + 2)
                    wait("summed", it + 1)
                    V.tensor_copy(scatter, bank[X0][:, 0:NT * P]).then_inc(S["scatter_taken"], 1)
                    wait("gate_tanh2", it + 1)
                    V.scalar_tensor_tensor(gate_t, gate_t, 1.0, bank[X0][:, :], ALU.add, ALU.mult).then_inc(S["gated"], 1)
                    wait("gated", it + 1)
                    wait("ring_free", it * PB + 2 * HK)
                    V.scalar_tensor_tensor(hid, gate_t, 0.5, bank[X1][:, :], ALU.mult, ALU.mult).then_inc(S["hid_ready"], 1)
                    wait("ring_free", it * PB + PB)
                    V.tensor_copy(y_sb[:, BW:2 * BW], bank[Y1][:, :]).then_inc(S["y_taken_dve"], 1)
                V.tensor_scalar(slot, slot, float(-SL), None, ALU.add).then_inc(S["slots_moved"], 1)
                wait("slots_moved", ps + 1)

            wait("sq3_done", 1)
            link(V.tensor_tensor(ss, e2[:, 0:2], e2[:, 2:4], ALU.add))
            tell(V.tensor_scalar(ss, ss, 1.0 / D, EPS, ALU.mult, ALU.add), "ss3_ready")
            wait("finw_loaded", 16)
            wait("rs3_ready")
            for t in range(NT):
                for n2 in range(2):
                    V.scalar_tensor_tensor(y_out[:, t, n2 * BW:(n2 + 1) * BW], acc[t][n2][:, :], rs[:, t:t + 1],
                                           fin_w[:, n2 * BW:(n2 + 1) * BW], ALU.mult, ALU.mult).then_inc(S["out_ready"], 1)

        @block.scalar
        def _(act):
            A = nc.scalar.activation

            def load(dst, src, name):
                act.dma_start(dst, src).then_inc(S[name], 16)

            def wait(name, n=1):
                act.wait_ge(*S.at(name, n))

            def tell(ins, name):
                ins.then_inc(S[name], 1)

            load(w_mix[:, :], mix_norm_w[0].rearrange("(p k) -> p k", k=KC), "mix_loaded")
            for n, o in ((RQ, 0), (RK, BW), (RV, 2 * BW)):
                load(prm_rows[n:n + TAPS, :], gdn_conv_w[0, :, o:o + BW], "prm_loaded")
            load(prm_rows[RC:RC + CTAPS, :], conf_conv_w[0], "prm_loaded")
            load(prm_rows[RS:RS + STAPS, :], sc_conv_w[0], "prm_loaded")
            for n, v in ((RCB, conf_conv_b), (RLW, conf_ln_w), (RLB, conf_ln_b)):
                load(prm_rows[n:n + 1, :], v, "prm_loaded")
            load(ws_sb, gmlp_w_s[0].rearrange("g i j -> i g j"), "ws_loaded")
            load(w_abs[:, :, :], w_in[0, :, OAB:OAB + 2 * H].rearrange("(p k) n -> p k n", k=KC), "wab_loaded")
            load(alog, gdn_A_log.to_broadcast([P, H]), "small_loaded")
            load(dtb, gdn_dt_bias.to_broadcast([P, H]), "small_loaded")
            load(w_gn, gdn_norm_w[0].rearrange("(p a) -> p a", a=1), "small_loaded")
            for t in range(NT):
                wait(f"x_loaded{t}", 16)
                tell(A(xn[:, t, :], x_sb[:, t, :], ACT.Square, accum_out=ss[:, t:t + 1]), "sq_done")
            wait("small_loaded", 48)
            tell(A(expA, alog, ACT.Exp), "expA_ready")
            wait("mix_loaded", 16)
            for b in range(2, 4):
                wait("xT_done", b + 1)
                for k in range(2 * b, 2 * b + 2):
                    ins = A(xnT[:, k, :], bank[b][:, (k % 2) * SEQ:(k % 2 + 1) * SEQ], ACT.Copy, scale=w_mix[:, k:k + 1])
                    if k % 2:
                        tell(ins, "xnT_act")
            wait("ab_done")
            ab = bank[Y0][:, 0:NT * 2 * H].rearrange("p (t c) -> p t c", t=NT)
            tell(A(th(beta), ab[:, :, 0:H], ACT.Tanh, scale=0.5), "beta_tanh")
            wait("abs_ready")
            tell(A(e3, e2, ACT.Exp, scale=-1.0), "exp_abs")
            wait("exp_abs")
            tell(A(e3, e3, ACT.Ln, bias=1.0), "log_ready")

            def copy_unit(m, h, dst):
                u = UNIT[m, h]
                wait("proj_done", u + 1)
                tell(A(dst, bank[u % 4][:, :].rearrange("p (c t) -> p c t", c=2), ACT.Copy), "proj_taken_act")

            wait("pads_ready")
            for h in range(2):
                copy_unit(PK, h, k_in[:, 2 * h:2 * h + 2, TAPS - 1:])
            wait("gc_taken")
            tell(A(egc, gcum, ACT.Exp), "egc_ready")
            wait("k_conv")
            tell(A(tan[0], k_ch, ACT.Tanh, scale=0.5), "k_tanh")
            wait("decay_taken", NT)
            for t in range(NT):
                v = egl.rearrange("p (t h b) -> p t h b", t=NT, h=H)[:, t]
                ins = A(v, bank4(X0 + t)[:, :, CH - 1::CH], ACT.Exp)
                if t:
                    tell(ins, "egl_ready")
            wait("gc_taken")
            tell(A(ekd, e2, ACT.Exp), "ekd_ready")
            for h in range(2):
                copy_unit(PQ, h, q_in[:, 2 * h:2 * h + 2, TAPS - 1:])
            wait("decay_log")
            tell(A(thf(10), thf(10), ACT.Exp, scale=-1.0), "decay_exp")
            wait("kf_done")
            for t in range(NT):
                ins = A(squares[:, t * H:(t + 1) * H, :], bank4(Y0 + t), ACT.Square)
                if t:
                    tell(ins, "sqk_done")
            wait("q_conv")
            wait("rows_done")
            tell(A(tan[1], q_ch, ACT.Tanh, scale=0.5), "q_tanh")
            for h in range(2):
                copy_unit(PV, h, v_in[:, 2 * h:2 * h + 2, TAPS - 1:])
            wait("qf_done")
            wait("ssk_ready")
            for t in range(NT):
                ins = A(squares[:, t * H:(t + 1) * H, :], bank4(X0 + t), ACT.Square)
                if t:
                    tell(ins, "sqq_done")
            wait("v_conv")
            wait("k_act")
            tell(A(tan[0], v_ch, ACT.Tanh, scale=0.5), "v_tanh")
            copy_unit(PCA, 0, conf_acc[:, 0:2, :])

            def take(done, dst0, dst, src, name):
                wait(*done)
                for t in range(NT):
                    ins = A(dst[:, t], bank4(src + t), ACT.Copy)
                    if t:
                        tell(ins, name)

            take(("kb_done", 1), 0, kT, Y0, "kT_ready")
            copy_unit(PCA, 1, conf_acc[:, 2:4, :])

            wait("q_act")
            for h in range(2):
                u = UNIT[PCG, h]
                wait("proj_done", u + 1)
                A(tan[1][:, 2 * h:2 * h + 2, :], bank[u % 4][:, :].rearrange("p (c t) -> p c t", c=2), ACT.Tanh,
                  scale=0.5).then_inc(S["proj_taken_act"], 1)
            take(("qb_done", 1), 0, qT, X0, "qT_ready")
            copy_unit(PSC, 0, workA[:, 0:2, :])
            take(("qdb_done", 1), 0, qdT, Y0, "qdT_ready")
            copy_unit(PSC, 1, workA[:, 2:4, :])
            take(("LT_done", 1), 0, Q_, Y0, "LT_taken")
            take(("AT_done", 1), 0, AT, X0, "AT_taken")
            load(ln_rows[:, 0, :], gmlp_ln_w.to_broadcast([P, BW]), "lnrows_loaded")
            load(ln_rows[:, 1, :], gmlp_ln_b.to_broadcast([P, BW]), "lnrows_loaded")

            def gate_unit(bi, g, h):
                m = (PG3A, PG2A, PG1A, PG0A)[bi] + g
                if bi > 1:
                    wait("gate_used", 4 * (bi - 2) + 2 * g + h + 1)
                u = UNIT[m, h]
                wait("proj_done", u + 1)
                A(tan[g][:, 2 * h:2 * h + 2, :], bank[u % 4][:, :].rearrange("p (c t) -> p c t", c=2), ACT.Tanh,
                  scale=0.5).then_inc(S["proj_taken_act"], 1)

            def take_u(n):
                take(("U_done", n), 0, U_, Y0, "U_taken")

            take_u(1)
            wait("v_act")
            wait("conf_in", 2)
            gate_unit(0, 0, 0)
            take_u(2)
            gate_unit(0, 0, 1)
            gate_unit(0, 1, 0)
            take_u(3)
            gate_unit(0, 1, 1)
            take_u(4)

            def gelu_act(n, m, h):
                u = UNIT[m, h]
                s = blk(16 + n // 2)[:, (n % 2) * 512:(n % 2 + 1) * 512]
                wait("proj_done", u + 1)
                if n == 0:
                    wait("proj_taken_dve", bank_free(UNIT[PW3, 3])[1])
                tell(A(s, bank[u % 4][:, :], ACT.Square), "gelu_sq")
                wait("gelu_in", n + 1)
                tell(A(s, s, ACT.Tanh, scale=0.7978845608028654), "gelu_tanh")

            gelu_act(0, PGV, 0)
            take_u(5)
            gelu_act(1, PGV, 1)
            wait("TUt_done", NM - 1)
            load(bs_row, gmlp_b_s[0].rearrange("g i -> (g i)").rearrange("(a n) -> a n", a=1).to_broadcast([P, BW]), "bs_loaded")
            gelu_act(2, PGU, 0)
            gelu_act(3, PGU, 1)
            take(("u_done", 1), 0, u_tok, X0, "u_taken")
            wait("gm_ln")
            take(("wT_done", 1), 0, wT, Y0, "wT_taken")
            for t in range(NT):
                load(x_res[:, t, :], x[0, t * P:(t + 1) * P, :], "xres_loaded")
            load(w_rt[:, :, 0:NG], router_grp[0].rearrange("(p k) e -> p k e", k=KC), "rt_loaded")
            load(w_rt[:, :, NG:], router_exp[0].rearrange("(p k) e -> p k e", k=KC), "rt_loaded")

            def take_o(c):
                t, b = divmod(c, P // CH)
                r = slice(b * CH, (b + 1) * CH)
                wait("o_done", c + 1)
                tell(A(o_tok[r, t], bank4(Y0)[r], ACT.Copy), "o_taken")

            take_o(0)
            wait("proj_taken_dve", bank_free(UNIT[PGU, 0])[1])
            gate_unit(1, 0, 0)
            wait("proj_taken_dve", bank_free(UNIT[PGU, 1])[1])
            gate_unit(1, 0, 1)
            take_o(1)
            wait("y2_ready")
            gate_unit(1, 1, 0)
            gate_unit(1, 1, 1)
            load(moe_w, moe_norm_w.to_broadcast([P, D]), "moew_loaded")
            take_o(2)
            for h in range(2):
                u = UNIT[PZ, h]
                wait("proj_done", u + 1)
                tell(A(zbuf[:, 2 * h:2 * h + 2, :], bank[u % 4][:, :].rearrange("p (c t) -> p c t", c=2), ACT.Tanh,
                       scale=0.5), "z_tanh")
            take_o(3)
            wait("o_taken", 4)
            tell(A(squares, thf(10), ACT.Square), "sqo_done")
            gate_unit(2, 0, 0)
            gate_unit(2, 0, 1)
            gate_unit(2, 1, 0)
            gate_unit(2, 1, 1)
            wait("cfB_done")
            for c in range(NCH):
                ins = A(conf_acc[:, c, :], bank[Y0 + c // 2][:, (c % 2) * SEQ:(c % 2 + 1) * SEQ], ACT.Identity,
                        bias=prm[:, c, RLB:RLB + 1], scale=prm[:, c, RLW:RLW + 1])
            tell(ins, "cf_tanh")
            wait("cf_tanh", 1)
            tell(A(cf_tok.rearrange("p t h d -> p (t h d)"), conf_acc.rearrange("p c t -> p (c t)"), ACT.Tanh), "cf_tanh")
            for g in range(2):
                for h in range(2):
                    gate_unit(3, g, h)
            wait("sso_ready")
            load(fin_w, final_norm_w.rearrange("(a n) -> a n", a=1).to_broadcast([P, D]), "finw_loaded")

            for t in range(NT):
                wait("proj_taken_dve", bank_free(UNIT[PO1, t])[1])
                tell(A(y_out[:, t, :], x2[:, t, :], ACT.Square, accum_out=ss[:, t:t + 1]), "sq2_done")
            for t in range(NT):
                wait("xmT_done", t + 1)
                tell(A(xmT[:, 0, :, t * P:(t + 1) * P], bank4(X0 + 2 * t), ACT.Copy), "xmT_act")
            r = [r8[:, n, :] for n in range(16)]
            for t in range(NT):
                wait("ngmax_ready", t + 1)
                A(r8e[:, :], lg[:, t, 0:NG], ACT.Exp, bias=r[4][:, 0:1], accum_out=r[4][:, 1:2])
                wait("gap_ready", t + 1)
                tell(A(r[10][:, 1:2], r[10][:, 0:1], ACT.Exp), "exps_done")

            wait("npass_ready")
            act.sem_inc(S["y_taken_act"], 1)
            act.sem_inc(S["hidT_taken"], 1)
            n = act.value_load(npass_i[0:1, 0:1], min_val=1, max_val=SEQ // SL)
            with act.Fori(0, n) as ps:
                with act.Fori(0, NB) as b:
                    it = ps * NB + b
                    wait("xg_done", it * 2 + 2)
                    A(xgT[:, 0:HK, :], bank4(Y0), ACT.Copy).then_inc(S["xg_taken_act"], 1)
                    wait("ring_free", it * PB + 2 * HK - 1)
                    A(gate_t, bank[X0][:, :], ACT.Tanh, scale=0.5).then_inc(S["gate_tanh2"], 1)
                    wait("hidT_done", it + 1)
                    A(hidT, bank4(X0), ACT.Copy).then_inc(S["hidT_taken"], 1)
                    wait("ring_free", it * PB + PB)
                    wait("summed", it + 1)
                    A(y_sb[:, 0:BW], bank[Y0][:, :], ACT.Copy).then_inc(S["y_taken_act"], 1)

            wait("sum_closed")
            for t in range(NT):
                for n2 in range(2):
                    ins = A(y_out[:, t, n2 * BW:(n2 + 1) * BW], acc[t][n2][:, :], ACT.Square,
                            accum_out=e2[:, t + NT * n2:t + NT * n2 + 1])
            tell(ins, "sq3_done")
            for t in range(NT):
                wait("out_ready", 2 * t + 2)
                act.dma_start(out[0, t * P:(t + 1) * P, :], y_out[:, t, :]).then_inc(S["out_stored"], 16)
            act.wait_ge(*S.at("out_stored", 16 * NT))


_INS = ['x', 'mix_norm_w', 'w_in', 'gdn_conv_w', 'gdn_A_log', 'gdn_dt_bias', 'gdn_norm_w', 'conf_conv_w',
        'conf_conv_b', 'conf_ln_w', 'conf_ln_b', 'gmlp_ln_w', 'gmlp_ln_b', 'gmlp_w_s', 'gmlp_b_s', 'sc_conv_w',
        'w_branch', 'w_out', 'moe_norm_w', 'router_grp', 'router_exp', 'w_gate', 'w_up', 'w_down', 'final_norm_w']


def kernel(**inputs):
    import numpy as _np
    import concourse.bacc as _bacc
    from concourse.bass_utils import run_bass_kernel_spmd as _run

    nc = _bacc.Bacc("TRN2", target_bir_lowering=False, num_devices=1)
    arrays, args = {}, []
    for name in _INS:
        a = _np.ascontiguousarray(inputs[name])
        arrays[f"in_{name}"] = a
        args.append(nc.dram_tensor(f"in_{name}", a.shape, mybir.dt.from_np(a.dtype), kind="ExternalInput").ap())
    out = nc.dram_tensor("out_x", inputs["x"].shape, mybir.dt.float32, kind="ExternalOutput").ap()
    hybrid_trunk_kernel(nc, *args, out)
    r = _run(nc, [arrays], core_ids=[0])
    return r.results[0]["out_x"]
```

```python
import concourse.bass as bass
from concourse import mybir
from contextlib import ExitStack


def hybrid_trunk_kernel(nc, x, mix_norm_w, w_in, gdn_conv_w, gdn_A_log, gdn_dt_bias, gdn_norm_w,
                        conf_conv_w, conf_conv_b, conf_ln_w, conf_ln_b, gmlp_ln_w, gmlp_ln_b,
                        gmlp_w_s, gmlp_b_s, sc_conv_w, w_branch, w_out, moe_norm_w, router_grp,
                        router_exp, w_gate, w_up, w_down, final_norm_w, out):
    f32 = mybir.dt.float32
    f32r = mybir.dt.float32r
    u32 = mybir.dt.uint32
    ALU = mybir.AluOpType
    ACT = mybir.ActivationFunctionType
    AXX = mybir.AxisListType.X

    P = 128
    _, SEQ, D = x.shape
    NT = SEQ // P
    KC = D // P
    BW = w_branch.shape[2]
    NCH = BW // P
    H = gdn_A_log.shape[1]
    CH = 64
    TAPS = gdn_conv_w.shape[1]
    CTAPS = conf_conv_w.shape[1]
    STAPS = sc_conv_w.shape[1]
    NG = router_grp.shape[2]
    NE = router_exp.shape[2]
    EG = NE // NG
    FE = w_gate.shape[3]
    FC = FE // P
    EPS = 1e-6
    EB = 4
    SL = P // EB
    NB = NE // EB
    HK = KC // 2
    PB = 2 * HK + FC

    R = 6
    RM = 8
    UB = 2
    NP = NB // UB
    PIECE = KC * BW

    OQ, OK, OV, OZ = 0, BW, 2 * BW, 3 * BW
    OAB = 4 * BW
    OCA = OAB + 2 * H
    OCG = OCA + BW
    OGU, OGV = OCG + BW, OCG + 2 * BW
    OSB, OSC, OSX = OGV + BW, OGV + 2 * BW, OGV + 3 * BW
    OG = OSX + BW

    def gate_cols(i, half):
        return ("in", OG + i * D + half * BW)

    FRONT = [("in", OK), ("in", OQ), ("in", OV), ("in", OCA), ("in", OCG),
             ("in", OSC), ("in", OSX), ("in", OSB), gate_cols(3, 0), gate_cols(3, 1), ("branch", 3),
             ("in", OGV), ("in", OGU), gate_cols(2, 0), gate_cols(2, 1), ("branch", 2),
             ("in", OZ), gate_cols(1, 0), gate_cols(1, 1), ("branch", 1),
             gate_cols(0, 0), gate_cols(0, 1), ("branch", 0), ("out", 0), ("out", BW)]
    (PK, PQ, PV, PCA, PCG, PSC, PSX, PSB, PG3A, PG3B, PW3, PGV, PGU, PG2A, PG2B, PW2,
     PZ, PG1A, PG1B, PW1, PG0A, PG0B, PW0, PO0, PO1) = range(len(FRONT))
    NF = len(FRONT)
    TOKEN_MAJOR = (PGV, PO0, PO1)
    EMPTIED_BY_ACT = (PK, PQ, PV, PCA, PCG, PSC, PG3A, PG3B, PG2A, PG2B, PG1A, PG1B, PG0A, PG0B)

    UNITS = [(m, h) for m in range(NF) for h in range(4 if FRONT[m][0] == "branch" else 2)]
    UNIT = {unit: u for u, unit in enumerate(UNITS)}

    NJ = 2 * NF
    NHI = 3
    LO_BY_DVE = (0, 1, 2)
    FRONT_SLOTS = (0, 1, 2, 4)

    def front_slot(m):
        return FRONT_SLOTS[(m - (NF - 4)) % 4]

    def front_full(m):
        return f"ring_full{front_slot(m)}", 16 * sum(1 for i in range(m + 1) if front_slot(i) == front_slot(m))

    FRONT_FULL = [16 * sum(1 for i in range(NF) if front_slot(i) == s) for s in range(R)]

    def job_used(j):
        m, h = divmod(j, 2)
        if m in TOKEN_MAJOR and h == 0:
            return "halves_used", TOKEN_MAJOR.index(m) + 1
        mine = [UNIT[unit] for unit in UNITS if unit[0] == m]
        return "proj_done", (mine[-1] if m in TOKEN_MAJOR else mine[(h + 1) * len(mine) // 2 - 1]) + 1

    def jobs_by(unit):
        m, h = unit
        units = 4 if FRONT[m][0] == "branch" else 2
        return 2 * m + (1 + h if m in TOKEN_MAJOR else (h + 1) * 2 // units)

    def lo_made(j):
        dve = j in LO_BY_DVE
        return ("lo_dve" if dve else "lo_pool"), sum(1 for i in range(j + 1) if (i in LO_BY_DVE) == dve)

    def units_through(m):
        return sum(1 for unit in UNITS if unit[0] <= m)

    def bank_free(u):
        act = UNITS[u][0] in EMPTIED_BY_ACT
        count = sum(1 for v in range(u + 1) if (UNITS[v][0] in EMPTIED_BY_ACT) == act)
        return ("proj_taken_act" if act else "proj_taken_dve"), count

    ctx = ExitStack()
    with ctx:
        def sb(name, shape, dt=f32):
            return ctx.enter_context(nc.sbuf_tensor(name, shape, dt))

        ONCE = {
            "pe_steps": ["prm_done", "ws_done", "ab_done", "gc_done", "rows_done", "kf_done", "qf_done", "kb_done",
                         "KK_done", "vf_done", "qb_done", "qdb_done", "QK_done", "LT_done", "AT_done", "u_done",
                         "wT_done", "mix_done", "cfT_done", "cfB_done", "oT_done", "counts_done", "sum_closed"],
            "dve_steps": ["ss_ready", "prm_taken", "ws_taken", "abs_ready", "ab_taken", "g_ready", "k_conv",
                          "gc_taken", "decay_log", "k_act", "q_conv", "ssk_ready", "q_act", "kbg_ready", "v_conv",
                          "ssq_ready", "v_act", "qd_ready", "kd_ready", "L_ready", "A_masked", "A_ready"],
        }

        class Signals(dict):
            def __missing__(self, name):
                for counter, events in ONCE.items():
                    if name in events:
                        self[name] = self[counter]
                        return self[name]
                self[name] = ctx.enter_context(nc.semaphore(name))
                return self[name]

            def at(self, name, n):
                for events in ONCE.values():
                    if name in events:
                        return self[name], events.index(name) + 1
                return self[name], n

        S = Signals()

        BLK = KC * P + 16
        NBLK = 20
        with (nc.sbuf_tensor("ring_parts", [P, R, PIECE], f32r) as ring_parts,
              nc.sbuf_tensor("arena_parts", [P, NBLK, BLK], f32r) as arena_parts):
            pass
        ring = sb("ring", [P, R, PIECE])
        arena = sb("arena", [P, NBLK, BLK])
        conf_pad = sb("conf_pad", [P, NCH, CTAPS - 1 + SEQ])

        def moe_slot(j):
            s = j % RM
            if s in (0, 3):
                n = 7 if s == 0 else 11
                return arena[:, n:n + 4, :].rearrange("p n c -> p (n c)")[:, 0:PIECE]
            return ring[:, s - 1 if s < 3 else s - 2, :]

        def moe_full(j):
            s = j % RM
            if s in (0, 3):
                return f"extra_full{s}", 0
            n = s - 1 if s < 3 else s - 2
            return f"ring_full{n}", FRONT_FULL[n]

        def hi_buffer(j):
            o = (j % NHI) * (PIECE // 2)
            return ring_parts[:, 5, o:o + PIECE // 2] if o < PIECE else ring_parts[:, 3, 0:PIECE // 2]

        def chunks(m):
            return NCH if FRONT[m][0] == "branch" else KC

        def hi_part(j):
            m = j // 2
            k = chunks(m) // 2 if m in TOKEN_MAJOR else chunks(m)
            return hi_buffer(j).rearrange("p (k n) -> p k n", k=k)

        def lo_part(j, of=ring_parts):
            m, h = divmod(j, 2)
            w = of[:, front_slot(m), :].rearrange("p (k n) -> p k n", k=chunks(m))
            if m in TOKEN_MAJOR:
                return w[:, h * chunks(m) // 2:(h + 1) * chunks(m) // 2, :]
            n = PIECE // chunks(m) // 2
            return w[:, :, h * n:(h + 1) * n]

        def weights(j):
            return lo_part(j, ring)

        def plain(a):
            return a.bitcast(f32)

        def blk(n, width=NCH * SEQ):
            return arena[:, n, 0:width]

        def cht(n):
            return blk(n).rearrange("p (c t) -> p c t", c=NCH)

        def tht(n):
            return blk(n).rearrange("p (t h d) -> p t h d", t=NT, h=H)

        def thf(n):
            return blk(n).rearrange("p (a d) -> p a d", d=P)

        def padded(n, pad):
            return blk(n, NCH * (pad + SEQ)).rearrange("p (c t) -> p c t", c=NCH)

        k_in, q_in, v_in = padded(0, TAPS - 1), padded(2, TAPS - 1), padded(4, TAPS - 1)
        k_ch, q_ch, v_ch = cht(1), cht(3), cht(5)
        k_tok, q_tok, vb_tok = tht(0), tht(2), tht(4)
        kbg_tok, qd_tok = tht(1), tht(3)
        kT, qT, qdT = tht(7), tht(8), tht(9)
        decay = tht(10)
        L_, QM, vn_tok = tht(11), tht(11), tht(11)
        Q_ = tht(12)
        A_, U_ = tht(13), tht(13)
        AT = tht(8)
        T_, V_ = tht(2), tht(3)
        u_tok = tht(5)
        wT = tht(7)
        o_tok = tht(10)
        x_sb = arena[:, 14:16, 0:D]
        xn = arena[:, 16:18, 0:D]
        xnT_hi = sb("xnT_hi", [P, KC, SEQ], f32r)
        xnT_lo = ring_parts[:, 3, PIECE // 2:].rearrange("p (k t) -> p k t", k=KC)
        src_hi = sb("src_hi", [P, NCH, SEQ], f32r)
        state = sb("state", [P, H, P])
        conf_acc = cht(6)
        workA, workB = cht(14), cht(15)
        cx = padded(15, STAPS - 1)
        tan = [cht(16), cht(17)]
        merged = arena[:, 18:20, 0:NCH * SEQ].rearrange("p b (c t) -> p b c t", c=NCH)

        def blk_lo(n):
            return arena_parts[:, n, 0:NCH * SEQ].rearrange("p (c t) -> p c t", c=NCH)

        BRANCH_LO = (blk_lo(14), blk_lo(6), blk_lo(15), blk_lo(14))
        merged_lo = arena_parts[:, 18:20, 0:NCH * SEQ].rearrange("p b (c t) -> p b c t", c=NCH)
        merged_hi = xnT_hi
        zbuf = cht(1)
        x_res = arena[:, 2:4, 0:D]
        ln_rows = blk(7).rearrange("p (n c) -> p n c", n=2)
        bs_row = blk(13)[:, 0:BW].rearrange("p (g i) -> p g i", g=H)
        g_wide = tht(17)
        cf_tok = tht(15)
        squares = thf(11)
        gm_v = arena[:, 14, 0:NT * BW].rearrange("p (t c) -> p t c", t=NT)
        gm_u = cht(15)

        ident = sb("ident", [P, P])
        ones = sb("ones", [P, P])
        up_incl = sb("up_incl", [P, P])
        lo_incl = sb("lo_incl", [P, P])
        lo_strict = sb("lo_strict", [P, P])
        same_chunk = sb("same_chunk", [P, P])
        NM = 6
        merge = sb("merge", [P, NM, P])
        merge_lo = sb("merge_lo", [P, P])
        prm = sb("prm", [P, NCH, 52])
        w_mix = sb("w_mix", [P, KC])
        w_abs = sb("w_abs", [P, KC, 2 * H])
        w_abs_hi = sb("w_abs_hi", [P, KC, 2 * H], f32r)
        w_abs_lo = sb("w_abs_lo", [P, KC, 2 * H], f32r)
        wcT = sb("wcT", [P, H, P])
        small = sb("small", [P, 256])
        NPRM = 3 * TAPS + CTAPS + STAPS + 3
        RQ, RK, RV = 0, TAPS, 2 * TAPS
        RC = 3 * TAPS
        RS = RC + CTAPS
        RCB = RS + STAPS
        RLW, RLB = RCB + 1, RCB + 2
        prm_rows = blk(13)[0:NPRM, 0:BW]
        ws_sb = blk(12)[:, 0:H * P].rearrange("p (g j) -> p g j", g=H)

        cursor = [0]

        def sm(n):
            a = cursor[0]
            cursor[0] += n
            return small[:, a:a + n]

        ss = sm(NT)
        rs = sm(NT)
        mhalf = sm(2 * NT * H)
        w_gn = sm(1)
        alog = sm(H)
        dtb = sm(H)
        expA = sm(H)
        beta = sm(NT * H)
        e1 = sm(NT * H)
        e2 = sm(NT * H)
        e3 = sm(NT * H)
        gl = sm(NT * H)
        egc = sm(NT * H)
        gcum = sm(NT * H)
        ekd = sm(NT * H)
        bgk = sm(NT * H)
        egl = sm(2 * NT * H)
        ssk, rk = sm(NT * H), sm(NT * H)
        ssq, rq = sm(NT * H), sm(NT * H)
        sso, ro = sm(NT * H), sm(NT * H)
        bnst = sm(6 * NT)
        mv = sm(2 * NT)
        rv = sm(NT)

        def th(a):
            return a.rearrange("p (t h) -> p t h", t=NT)

        bank = [ctx.enter_context(nc.psum_tensor(f"bank{i}", [P, 512], f32)) for i in range(8)]

        def bank4(b):
            return bank[b][:, :].rearrange("p (h d) -> p h d", h=4)

        X0, X1, Y0, Y1 = 4, 5, 6, 7

        x2 = arena[:, 2:4, 0:D]
        xm = arena[:, 4:6, 0:D]
        xmT = arena[:, 0:2, 0:D].rearrange("p a (k t) -> p a k t", k=HK)
        xgT = blk(6).rearrange("p (k s) -> p k s", k=KC)
        gate_t = blk(0)[:, 0:FE]
        hid = blk(0)[:, FE:2 * FE]
        hidT = blk(1)[:, 0:FE].rearrange("p (j s) -> p j s", j=FC)
        y_sb = blk(16)
        moe_w = arena[:, 16, 0:D]
        fin_w = arena[:, 15, 0:D]
        w_rt = blk(17)[:, 0:KC * (NG + NE)].rearrange("p (k e) -> p k e", k=KC)
        tabs = blk(19)[:, 0:4 * NT * NE].rearrange("p (n t e) -> p n t e", n=4, t=NT)
        assigned, weight, slot, tmp64 = tabs[:, 0], tabs[:, 1], tabs[:, 2], tabs[:, 3]
        onehot = blk(17)[:, 0:NT * P].rearrange("p (t e s) -> p t e s", t=NT, e=EB)
        onehot_w = blk(17)[:, NT * P:2 * NT * P].rearrange("p (t e s) -> p t e s", t=NT, e=EB)
        scatter = blk(18)[:, 0:NT * P]
        lg = blk(18)[:, 512:512 + NT * (NG + NE)].rearrange("p (t e) -> p t e", t=NT)
        zero_w = conf_pad[:, 2, 0:P // 2].bitcast(mybir.dt.bfloat16)
        zero_x = conf_pad[:, 3, 0:BW // 2].bitcast(mybir.dt.bfloat16)
        upper_strict = sb("upper_strict", [P, P])
        iota_s = sb("iota_s", [P, SL])
        npass_f = sb("npass_f", [P, 8])
        npass_i = sb("npass_i", [P, 2], mybir.dt.int32)
        acc = [[bank[2 * t + n] for n in range(2)] for t in range(NT)]
        y_out = arena[:, 2:4, 0:D]
        sq_out = arena[:, 0:2, 0:D]
        r8 = conf_pad[:, 1, 0:16 * NT * 8].rearrange("p (n t e) -> p n t e", t=NT, e=8)
        best_index = sb("best_index", [P, 2, NT, 8], u32)
        grp_exp = sb("grp_exp", [P, NT, NG])

        block = ctx.enter_context(nc.Block())

        @block.sync
        def _(sp):
            for t in range(NT):
                sp.dma_start(x_sb[:, t, :], x[0, t * P:(t + 1) * P, :]).then_inc(S[f"x_loaded{t}"], 16)
            for m, (kind, c) in enumerate(FRONT):
                slot_m = ring[:, front_slot(m), :]
                if m >= 4:
                    sp.wait_ge(*S.at("proj_done", units_through(m - 4)))
                if kind == "in":
                    src = w_in[0, :, c:c + BW].rearrange("(p k) n -> p k n", k=KC)
                    dst = slot_m.rearrange("p (k n) -> p k n", k=KC)
                elif kind == "branch":
                    src = w_branch[0, c].rearrange("(k p) n -> p k n", p=P)
                    dst = slot_m.rearrange("p (k n) -> p k n", k=NCH)
                else:
                    src = w_out[0, :, c:c + BW].rearrange("(k p) n -> p k n", p=P)
                    dst = slot_m.rearrange("p (k n) -> p k n", k=KC)
                sp.dma_start(dst, src).then_inc(S[f"ring_full{front_slot(m)}"], 16)
                if m == 0:
                    for n, o in ((RQ, 0), (RK, BW), (RV, 2 * BW)):
                        sp.dma_start(prm_rows[n:n + TAPS, :], gdn_conv_w[0, :, o:o + BW]).then_inc(S["prm_loaded"], 16)
                    sp.dma_start(prm_rows[RC:RC + CTAPS, :], conf_conv_w[0]).then_inc(S["prm_loaded"], 16)
                    sp.dma_start(prm_rows[RS:RS + STAPS, :], sc_conv_w[0]).then_inc(S["prm_loaded"], 16)
                    for n, v in ((RCB, conf_conv_b), (RLW, conf_ln_w), (RLB, conf_ln_b)):
                        sp.dma_start(prm_rows[n:n + 1, :], v).then_inc(S["prm_loaded"], 16)
                    sp.dma_start(ws_sb, gmlp_w_s[0].rearrange("g i j -> i g j")).then_inc(S["ws_loaded"], 16)

            FREED_BY = (None, NF - 4, NF - 3, PW0, NF - 2, NF - 2, NF - 1, NF - 1)

            def pair(itp, bp, first=False):
                for i in range(UB * PB):
                    half, j = divmod(i, PB)
                    experts = bass.ds((bp * UB + half) * EB, EB)
                    dst = moe_slot(i)
                    if j < 2 * HK:
                        w = w_up if j % 2 else w_gate
                        kp = j // 2
                        src = w[0, experts].rearrange("e (p k) n -> p e k n", k=KC)[:, :, 2 * kp:2 * kp + 2, :]
                        dst = dst.rearrange("p (e k n) -> p e k n", e=EB, k=2)
                    else:
                        src = w_down[0, experts].rearrange("e (p j) n -> p e j n", j=FC)[:, :, j - 2 * HK, :]
                        dst = dst.rearrange("p (e n) -> p e n", e=EB)
                    if not first or i >= RM:
                        sp.wait_ge(*S.at("ring_free", itp * (UB * PB) + (i - RM + 1)))
                    elif FREED_BY[i] is None:
                        sp.wait_ge(*S.at("oT_done", 1))
                    else:
                        sp.wait_ge(*S.at("proj_done", units_through(FREED_BY[i])))
                    sp.dma_start(dst, src).then_inc(S[moe_full(i)[0]], 16)

            pair(0, 0, first=True)
            with sp.Fori(1, NP) as bp:
                pair(bp, bp)
            sp.wait_ge(*S.at("npass_ready", 1))
            n = sp.value_load(npass_i[0:1, 0:1], min_val=1, max_val=SEQ // SL)
            with sp.If(n > 1):
                with sp.Fori(1, n) as ps:
                    with sp.Fori(0, NP) as bp:
                        pair(ps * NP + bp, bp)

        @block.gpsimd
        def _(pool):
            made = [0]

            def put(ins):
                made[0] += 1
                ins.then_inc(S["pool_chain"], 1)
                pool.wait_ge(*S.at("pool_chain", made[0]))

            def keep(t, pattern, base, cm, op=ALU.is_ge, fill=0.0):
                put(nc.gpsimd.affine_select(out=t, in_=t, compare_op=op, fill=fill, base=base,
                                            pattern=pattern, channel_multiplier=cm))

            NCK = P // CH

            def in_chunk(t):
                v = t.rearrange("p (b c) -> p b c", c=CH)
                keep(v, [[-CH, NCK], [0, CH]], 0, 1)
                keep(v, [[CH, NCK], [0, CH]], CH - 1, -1)

            put(nc.gpsimd.memset(ident[:, :], 0.0))
            keep(ident[:, :], [[-1, P]], 0, 1, ALU.not_equal, 1.0)
            nc.gpsimd.memset(ones[:, :], 1.0).then_inc(S["ident_ready"], 1)
            nc.gpsimd.memset(mhalf, -0.5)
            put(nc.gpsimd.memset(same_chunk[:, :], 1.0))
            in_chunk(same_chunk[:, :])
            pool.wait_ge(*S.at("ss_ready", 1))
            nc.gpsimd.tensor_tensor(rs, ss, mhalf[:, 0:NT], ALU.pow).then_inc(S["rs_ready"], 1)
            for t in (k_in, q_in, v_in):
                nc.gpsimd.memset(t[:, :, 0:TAPS - 1], 0.0)
            put(nc.gpsimd.memset(conf_pad[:, :, 0:CTAPS - 1], 0.0))
            for t, sign, strict in ((up_incl, 1, 0), (lo_incl, -1, 0), (lo_strict, -1, 1)):
                put(nc.gpsimd.tensor_copy(t[:, :], same_chunk[:, :]))
                keep(t[:, :], [[sign, P]], -strict, -sign)
            pool.sem_inc(S["pads_ready"], 1)
            put(nc.gpsimd.memset(merge[:, :, :], 0.0))
            put(nc.gpsimd.memset(merge_lo[:, :], 0.0))
            for n in range(NM):
                s = 1 << n
                v = merge[:, n, :].rearrange("p (b h c) -> p b h c", h=2, c=s)[:, :, 1, :]
                put(nc.gpsimd.memset(v, 1.0))
                keep(v, [[-2 * s, P // (2 * s)], [0, s]], 0, 1)
                keep(v, [[2 * s, P // (2 * s)], [0, s]], s - 1, -1)
            keep(merge_lo[:, :].rearrange("p (b h) -> p b h", h=2)[:, :, 0], [[-2, P // 2]], -1, 1,
                 ALU.not_equal, 1.0)
            put(nc.gpsimd.memset(upper_strict[:, :], 1.0))
            keep(upper_strict[:, :], [[1, P]], -1, -1)
            put(nc.gpsimd.iota(iota_s[:, :], pattern=[[1, SL]], base=0, channel_multiplier=0,
                               allow_small_or_imprecise_dtypes=True))
            pool.sem_inc(S["masks_ready"], 1)
            def split_lo(first, last):
                for j in range(2 * first, 2 * last + 2):
                    if j not in LO_BY_DVE:
                        pool.wait_ge(*S.at("hi_ready", j))
                        nc.gpsimd.tensor_tensor(lo_part(j), weights(j), plain(hi_part(j)),
                                                ALU.subtract).then_inc(S["lo_pool"], 1)

            pool.wait_ge(*S.at("ws_taken", 1))
            nc.gpsimd.affine_select(out=wcT[:, :, :], in_=wcT[:, :, :], compare_op=ALU.is_ge, fill=0.0, base=0,
                                    pattern=[[0, H], [1, P]], channel_multiplier=-1).then_inc(S["wc_ready"], 1)
            def power(ready, done, dst, src):
                pool.wait_ge(*S.at(ready, 1))
                nc.gpsimd.tensor_tensor(dst, src, mhalf[:, 0:src.shape[-1]], ALU.pow).then_inc(S[done], 1)

            split_lo(PQ, PV)
            power("ssk_ready", "rk_ready", rk, ssk)
            split_lo(PCA, PCA)
            power("ssq_ready", "rq_ready", rq, ssq)
            split_lo(PCG, PGU)
            power("gm_var", "gm_rstd", rv, rv)
            split_lo(PG2A, PG1A)
            power("sso_ready", "ro_ready", ro, sso)
            power("cf_var", "cf_rstd", rv, rv)
            split_lo(PG1B, PO1)
            for t in range(NT):
                pool.wait_ge(*S.at("ss2_ready", t + 1))
                nc.gpsimd.tensor_tensor(rs[:, t:t + 1], ss[:, t:t + 1], mhalf[:, 0:1],
                                        ALU.pow).then_inc(S["rs2_ready"], 1)
            pool.wait_ge(*S.at("ss3_ready", 1))
            nc.gpsimd.tensor_tensor(rs, ss, mhalf[:, 0:NT], ALU.pow).then_inc(S["rs3_ready"], 1)

        @block.tensor
        def _(pe):
            mm = nc.tensor.matmul

            def unit(m, h):
                u = UNIT[m, h]
                kind, c0 = FRONT[m]
                dst = bank[u % 4]
                q = h * 2 // (4 if kind == "branch" else 2)
                if h in (0, 1 if kind != "branch" else 2):
                    pe.wait_ge(*S.at(*lo_made(2 * m + q)))
                if u >= 4:
                    name, count = bank_free(u - 4)
                    pe.wait_ge(*S.at(name, count))
                nk = NCH if kind == "branch" else KC
                src_h, src_l = (src_hi, BRANCH_LO[c0]) if kind == "branch" else (xnT_hi, xnT_lo)
                j = 2 * m + q
                for c in range(2):
                    o = ((2 * h + c) * P) % (PIECE // nk // 2)
                    out_c = dst[:, c * SEQ:(c + 1) * SEQ]
                    for k in range(nk):
                        if u == 0 and c == 0 and k % 2 == 0:
                            pe.wait_ge(*S.at("xnT_split", k // 2 + 1))
                        w_h, w_l = hi_part(j)[:, k, o:o + P], lo_part(j)[:, k, o:o + P]
                        x_h, x_l = src_h[:, k, :], src_l[:, k, :]
                        mm(out_c, w_h, x_h, start=k == 0, stop=False)
                        mm(out_c, w_h, x_l, start=False, stop=False)
                        last = mm(out_c, w_l, x_h, start=False, stop=k == nk - 1)
                last.then_inc(S["proj_done"], 1)

            def token_piece(m):
                for half in range(2):
                    j = 2 * m + half
                    pe.wait_ge(*S.at(*lo_made(j)))
                    for t in range(NT):
                        u = UNIT[m, t]
                        dst = bank[u % 4]
                        if half == 0:
                            name, count = bank_free(u - 4)
                            pe.wait_ge(*S.at(name, count))
                        tokens = slice(t * P, (t + 1) * P)
                        for kj in range(KC // 2):
                            k = half * (KC // 2) + kj
                            if m == PO0 and t == 0 and k % 2 == 0:
                                pe.wait_ge(*S.at("merged_split", k // 2 + 1))
                            if m == PGV:
                                t_h, t_l = xnT_hi[:, k, tokens], xnT_lo[:, k, tokens]
                            else:
                                t_h, t_l = merged_hi[:, k, tokens], merged_lo[:, k // NCH, k % NCH, tokens]
                            w_h, w_l = hi_part(j)[:, kj, :], lo_part(j)[:, kj, :]
                            mm(dst[:, :], t_h, w_h, start=k == 0, stop=False)
                            mm(dst[:, :], t_h, w_l, start=False, stop=False)
                            last = mm(dst[:, :], t_l, w_h, start=False, stop=k == KC - 1)
                        if half:
                            last.then_inc(S["proj_done"], 1)
                    if half == 0:
                        last.then_inc(S["halves_used"], 1)

            def tr(dst, src, n=P):
                return nc.tensor.transpose(dst, src, ident[0:n, 0:n])

            pe.wait_ge(*S.at("ident_ready", 1))
            pe.wait_ge(*S.at("xn_ready", NT))
            for k in range(KC):
                for t in range(NT):
                    last = tr(bank[k // 2][:, (k % 2) * SEQ + t * P:(k % 2) * SEQ + (t + 1) * P], xn[:, t, k::KC])
                if k % 2:
                    last.then_inc(S["xT_done"], 1)
            def parameters():
                pe.wait_ge(*S.at("prm_loaded", 16 * 8))
                for c in range(NCH):
                    last = tr(bank[X0][:, c * 52:c * 52 + NPRM], prm_rows[:, c * P:(c + 1) * P], NPRM)
                last.then_inc(S["prm_done"], 1)
                pe.wait_ge(*S.at("ws_loaded", 16))
                for g in range(H):
                    last = tr(bank4(X1)[:, g, :], ws_sb[:, g, :])
                last.then_inc(S["ws_done"], 1)

            def beta_and_g():
                pe.wait_ge(*S.at("wab_split", 2))
                for t in range(NT):
                    ab_t = bank[Y0][:, t * 2 * H:(t + 1) * 2 * H]
                    for k in range(KC):
                        x_h, x_l = (v[:, k, t * P:(t + 1) * P] for v in (xnT_hi, xnT_lo))
                        w_h, w_l = w_abs_hi[:, k, :], w_abs_lo[:, k, :]
                        mm(ab_t, x_h, w_h, start=k == 0, stop=False)
                        mm(ab_t, x_h, w_l, start=False, stop=False)
                        last = mm(ab_t, x_l, w_h, start=False, stop=k == KC - 1)
                last.then_inc(S["ab_done"], 1)

            def decays():
                pe.wait_ge(*S.at("g_ready", 1))
                pe.wait_ge(*S.at("pads_ready", 1))
                for t in range(NT):
                    g_t = th(gl)[:, t, :]
                    mm(bank[Y1][:, t * 2 * H:t * 2 * H + H], up_incl[:, :], g_t, start=True, stop=True)
                    last = mm(bank[Y1][:, t * 2 * H + H:(t + 1) * 2 * H], same_chunk[:, :], g_t,
                              start=True, stop=True)
                last.then_inc(S["gc_done"], 1)
                pe.wait_ge(*S.at("prm_taken", 1))
                pe.wait_ge(*S.at("ws_taken", 1))
                for t in range(NT):
                    for h in range(H):
                        last = mm(bank4(X0 + t)[:, h, :], g_wide[:, t, h, :], up_incl[:, :], start=True, stop=True)
                last.then_inc(S["rows_done"], 1)

            COUNTS = {"kn_ready": NT, "qn_ready": NT, "vb_ready": NT, "decay_taken": NT, "KK_taken": NT * H}

            def transposes(ready, taken, done, dst0, src):
                pe.wait_ge(*S.at(ready, COUNTS.get(ready, 1)))
                for name in taken:
                    pe.wait_ge(*S.at(name, COUNTS.get(name, 1)))
                for t in range(NT):
                    for h in range(H):
                        last = tr(bank4(dst0 + t)[:, h, :], src(t, h))
                last.then_inc(S[done], 1)

            def products(waits, done, dst0, lhsT, rhs):
                for name, n in waits:
                    pe.wait_ge(*S.at(name, n))
                for t in range(NT):
                    for h in range(H):
                        last = mm(bank4(dst0 + t)[:, h, :], lhsT[:, t, h, :], rhs[:, t, h, :], start=True, stop=True)
                last.then_inc(S[done], 1)

            def merge_u(n):
                products([("QM_ready", n), ("T_ready", n), ("LT_taken" if n == 1 else "W_taken", 1 if n == 1 else n - 1)],
                         "U_done", Y0, QM, T_)

            def merge_w(n):
                waits = [("U_taken", n), ("AT_taken" if n == 1 else "W_taken", 1 if n == 1 else n - 1)]
                if n < NM - 1:
                    products(waits, "TU_done", X0, V_, U_)
                products(waits, "TUt_done", Y0, U_, V_)

            def solve():
                products([("vb_ready", NT), ("W_taken", NM - 1)], "u_done", X0, V_, vb_tok)
                products([("kbg_ready", 1)], "wT_done", Y0, kbg_tok, V_)

            def chunk_v(c):
                t, b = divmod(c, P // CH)
                r = slice(b * CH, (b + 1) * CH)
                pe.wait_ge(*S.at("wT_taken", 1))
                pe.wait_ge(*S.at("u_taken", 1))
                pe.wait_ge(*S.at("state_ready", c))
                pe.wait_ge(*S.at("mix_taken", NCH))
                for h in range(H):
                    last = mm(bank4(X0 + t)[r, h, :], wT[:, t, h, r], state[:, h, :], start=True, stop=True)
                last.then_inc(S["ws_state"], 1)

            def chunk_o(c):
                t, b = divmod(c, P // CH)
                r = slice(b * CH, (b + 1) * CH)
                pe.wait_ge(*S.at("vn_ready", c + 1))
                pe.wait_ge(*S.at("wT_taken", 1))
                pe.wait_ge(*S.at("kd_ready", 1))
                if c:
                    pe.wait_ge(*S.at("o_taken", c))
                    pe.wait_ge(*S.at("state_ready", c))
                for h in range(H):
                    if c:
                        mm(bank4(Y0)[r, h, :], qdT[:, t, h, r], state[:, h, :], start=True, stop=False)
                    last = mm(bank4(Y0)[r, h, :], AT[r, t, h, r], vn_tok[r, t, h, :], start=c == 0, stop=True)
                last.then_inc(S["o_done"], 1)
                if c < 3:
                    for h in range(H):
                        last = mm(bank4(Y1)[:, h, :], k_tok[r, t, h, :], vn_tok[r, t, h, :], start=True, stop=True)
                    last.then_inc(S["state_add"], 1)

            def mixed():
                pe.wait_ge(*S.at("gm_ln", 1))
                pe.wait_ge(*S.at("wc_ready", 1))
                pe.wait_ge(*S.at("u_taken", 1))
                for g in range(H):
                    for t in range(NT):
                        o = (g % 2) * SEQ + t * P
                        last = mm(bank[X0 + g // 2][:, o:o + P], gm_v[:, t, g * P:(g + 1) * P], wcT[:, g, :],
                                  start=True, stop=True)
                last.then_inc(S["mix_done"], 1)

            def conf_fwd():
                pe.wait_ge(*S.at("cf_conv", NCH))
                pe.wait_ge(*S.at("o_taken", 4))
                pe.wait_ge(*S.at("state_ready", 3))
                for t in range(NT):
                    for c in range(NCH):
                        last = tr(bank4(Y0 + t)[:, c, :], conf_acc[:, c, t * P:(t + 1) * P])
                last.then_inc(S["cfT_done"], 1)

            def conf_back():
                pe.wait_ge(*S.at("cf_norm", NT))
                for c in range(NCH):
                    for t in range(NT):
                        last = tr(bank[Y0 + c // 2][:, (c % 2) * SEQ + t * P:(c % 2) * SEQ + (t + 1) * P],
                                  cf_tok[:, t, c, :])
                last.then_inc(S["cfB_done"], 1)

            def o_back():
                pe.wait_ge(*S.at("on_ready", 1))
                for h in range(H):
                    for t in range(NT):
                        last = tr(bank[X0 + h // 2][:, (h % 2) * SEQ + t * P:(h % 2) * SEQ + (t + 1) * P],
                                  o_tok[:, t, h, :])
                last.then_inc(S["oT_done"], 1)

            after = {
                (PK, 0): [parameters, beta_and_g],
                (PQ, 0): [decays],
                (PQ, 1): [lambda: transposes("k_act", ("ab_taken", "gc_taken", "egc_ready"), "kf_done", Y0, lambda t, h: k_ch[:, h, t * P:(t + 1) * P])],
                (PV, 1): [lambda: transposes("q_act", ("decay_taken", "egl_ready"), "qf_done", X0, lambda t, h: q_ch[:, h, t * P:(t + 1) * P])],
                (PCA, 0): [lambda: transposes("kn_ready", ("sqk_done",), "kb_done", Y0, lambda t, h: k_tok[:, t, h, :])],
                (PCA, 1): [lambda: products([("kT_ready", 1)], "KK_done", Y0, kT, kT)],
                (PCG, 0): [lambda: transposes("v_act", ("qn_ready",), "vf_done", X0, lambda t, h: v_ch[:, h, t * P:(t + 1) * P])],
                (PCG, 1): [lambda: transposes("qn_ready", ("vb_ready",), "qb_done", X0, lambda t, h: q_tok[:, t, h, :])],
                (PSC, 0): [lambda: transposes("qd_ready", ("KK_taken",), "qdb_done", Y0, lambda t, h: qd_tok[:, t, h, :])],
                (PSC, 1): [lambda: products([("qT_ready", 1)], "QK_done", X0, qT, kT)],
                (PSX, 0): [lambda: transposes("L_ready", ("qdT_ready",), "LT_done", Y0, lambda t, h: L_[:, t, h, :])],
                (PSX, 1): [lambda: transposes("A_ready", (), "AT_done", X0, lambda t, h: A_[:, t, h, :])],
                (PSB, 0): [lambda: merge_u(1)], (PSB, 1): [lambda: merge_w(1)],
                (PG3A, 0): [lambda: merge_u(2)], (PG3A, 1): [lambda: merge_w(2)],
                (PG3B, 0): [lambda: merge_u(3)], (PG3B, 1): [lambda: merge_w(3)],
                (PW3, 1): [lambda: merge_u(4)], (PW3, 3): [lambda: merge_w(4)],
                (PGV, 0): [lambda: merge_u(5)], (PGV, 1): [lambda: merge_w(5)],
                (PGU, 1): [solve],
                (PG2A, 0): [lambda: chunk_o(0), mixed],
                (PG2A, 1): [lambda: chunk_v(1)],
                (PG2B, 0): [lambda: chunk_o(1)],
                (PW2, 0): [lambda: chunk_v(2)],
                (PW2, 3): [lambda: chunk_o(2)],
                (PZ, 0): [lambda: chunk_v(3)],
                (PZ, 1): [lambda: chunk_o(3)],
                (PG1A, 0): [conf_fwd],
                (PG1A, 1): [conf_back],
                (PG1B, 0): [o_back],
            }
            for u, key in enumerate(UNITS):
                if key in ((PW3, 0), (PW2, 0), (PW1, 0), (PW0, 0)):
                    pe.wait_ge(*S.at("y_split", 1 + (PW3, PW2, PW1, PW0).index(key[0])))
                if key[0] not in TOKEN_MAJOR:
                    unit(*key)
                elif key[1] == 0:
                    token_piece(key[0])
                for step in after.get(key, []):
                    step()

            pe.wait_ge(*S.at("proj_taken_dve", bank_free(len(UNITS) - 1)[1]))
            for t in range(NT):
                for n in range(2):
                    last = mm(acc[t][n][:, :], ident[:, :], x2[:, t, n * BW:(n + 1) * BW], start=True, stop=False)
            for t in range(NT):
                pe.wait_ge(*S.at("xm_ready", t + 1))
                for k in range(KC):
                    last = tr(bank4(X0 + 2 * t + k // HK)[:, k % HK, :], xm[:, t, k * P:(k + 1) * P])
                last.then_inc(S["xmT_done"], 1)
            pe.wait_ge(*S.at("rt_loaded", 16 * 2))
            for t in range(NT):
                pe.wait_ge(*S.at("xmT_act", t + 1))
                pe.wait_ge(*S.at("xmT_dve", t + 1))
                for k in range(KC):
                    last = mm(bank[X0][:, t * (NG + NE):(t + 1) * (NG + NE)], xmT[:, k // HK, k % HK, t * P:(t + 1) * P],
                              w_rt[:, k, :], start=k == 0, stop=k == KC - 1)
                last.then_inc(S["logits_done"], 1)
            pe.wait_ge(*S.at("assigned_ready", 1))
            for t in range(NT):
                for s in range(t):
                    mm(bank[Y0][:, t * NE:(t + 1) * NE], ones[:, :], assigned[:, s, :], start=s == 0, stop=False)
                last = mm(bank[Y0][:, t * NE:(t + 1) * NE], upper_strict[:, :], assigned[:, t, :],
                          start=t == 0, stop=True)
            for t in range(NT):
                last = mm(bank[Y1][:, 0:NE], ones[:, :], assigned[:, t, :], start=t == 0, stop=t == NT - 1)
            last.then_inc(S["counts_done"], 1)

            pe.wait_ge(*S.at("npass_ready", 1))
            pe.sem_inc(S["xg_done"], 1)
            pe.sem_inc(S["scatter_done"], 1)
            pe.sem_inc(S["summed"], 1)
            n = pe.value_load(npass_i[0:1, 0:1], min_val=1, max_val=SEQ // SL)
            with pe.Fori(0, n) as ps:
                with pe.Fori(0, NP) as bp:
                    def full(i):
                        name, before = moe_full(i)
                        return S.at(name, (ps * NP + bp) * (16 * UB * PB // RM) + before + 16 * (i // RM + 1))

                    for half in range(UB):
                        b = bp * UB + half
                        it = ps * NB + b
                        pe.wait_ge(*S.at("onehot_ready", it + 1))
                        pe.wait_ge(*S.at("y_taken_act", it + 1))
                        pe.wait_ge(*S.at("y_taken_dve", it + 1))
                        for k in range(KC):
                            for t in range(NT):
                                last = mm(bank4(Y0 + k // HK)[:, k % HK, :], xm[:, t, k * P:(k + 1) * P],
                                          onehot[:, t].rearrange("p e s -> p (e s)"), start=t == 0, stop=t == NT - 1)
                            if k % HK == HK - 1:
                                last.then_inc(S["xg_done"], 1)
                        pe.wait_ge(*S.at("hidT_taken", it + 1))
                        pe.wait_ge(*S.at("onehot_w_ready", it + 1))
                        for t in range(NT):
                            last = tr(bank[X0][:, t * P:(t + 1) * P], onehot_w[:, t].rearrange("p e s -> p (e s)"))
                        last.then_inc(S["scatter_done"], 1)
                        pe.wait_ge(*S.at("scatter_taken", it + 1))
                        for j in range(2 * HK):
                            w = moe_slot(half * PB + j).rearrange("p (e k n) -> p e k n", e=EB, k=2)
                            dst = bank[X1] if j % 2 else bank[X0]
                            if j == 0:
                                pe.wait_ge(*S.at("xg_taken_act", it + 1))
                                pe.wait_ge(*S.at("xg_taken_dve", it + 1))
                            pe.wait_ge(*full(half * PB + j))
                            for kk in range(2):
                                k = 2 * (j // 2) + kk
                                for e in range(EB):
                                    rows = slice(e * SL, (e + 1) * SL)
                                    last = mm(dst[rows, :], xgT[:, k, rows], w[:, e, kk, :],
                                              start=k == 0, stop=k == KC - 1)
                            last.then_inc(S["ring_free"], 1)
                        pe.wait_ge(*S.at("hid_ready", it + 1))
                        for j in range(FC):
                            last = tr(bank4(X0)[:, j, :], hid[:, j::FC])
                        last.then_inc(S["hidT_done"], 1)
                        pe.wait_ge(*S.at("hidT_taken", it + 2))
                        for j in range(FC):
                            w = moe_slot(half * PB + 2 * HK + j).rearrange("p (e n) -> p e n", e=EB)
                            pe.wait_ge(*full(half * PB + 2 * HK + j))
                            for n2 in range(2):
                                for e in range(EB):
                                    rows = slice(e * SL, (e + 1) * SL)
                                    last = mm(bank[Y0 + n2][rows, :], hidT[:, j, rows],
                                              w[:, e, n2 * BW:(n2 + 1) * BW], start=j == 0, stop=j == FC - 1)
                                if j == FC - 1 and n2 == 0:
                                    last.then_inc(S["y_half_done"], 1)
                            last.then_inc(S["ring_free"], 1)
                        for n2 in range(2):
                            pe.wait_ge(*S.at("y_taken_dve" if n2 else "y_taken_act", it + 2))
                            for t in range(NT):
                                last = mm(acc[t][n2][:, :], scatter[:, t * P:(t + 1) * P],
                                          y_sb[:, n2 * BW:(n2 + 1) * BW], start=False, stop=False)
                        last.then_inc(S["summed"], 1)
            for t in range(NT):
                for n2 in range(2):
                    last = mm(acc[t][n2][:, :], zero_w, zero_x, start=False, stop=True)
            last.then_inc(S["sum_closed"], 1)

        @block.vector
        def _(dve):
            V = nc.vector
            made = [0]

            def do(ins):
                made[0] += 1
                ins.then_inc(S["dve_chain"], 1)
                return made[0]

            def need(n):
                dve.wait_ge(*S.at("dve_chain", n))

            def link(ins):
                need(do(ins))

            def tell(ins, name):
                ins.then_inc(S[name], 1)

            def wait(name, n=1):
                dve.wait_ge(*S.at(name, n))

            def wide(v, n):
                return v.unsqueeze(2).to_broadcast([P, v.shape[1], n])

            def rows(m, n):
                return m.unsqueeze(1).to_broadcast([P, n, m.shape[-1]])

            def conv(src, dst, row, taps, name=None, chunks=range(NCH), first=0, last=None):
                last = taps if last is None else last
                at = {}
                for j in range(first, last):
                    for c in chunks:
                        x_j = src[:, c, j:j + SEQ]
                        w_j = prm[:, c, row + j:row + j + 1]
                        if c in at:
                            need(at[c])
                        if j == 0:
                            ins = V.tensor_scalar(dst[:, c, :], x_j, w_j, None, ALU.mult)
                        else:
                            ins = V.scalar_tensor_tensor(dst[:, c, :], x_j, w_j, dst[:, c, :], ALU.mult, ALU.add)
                        if name and j == last - 1 and c == chunks[-1]:
                            tell(ins, name)
                            wait(name)
                        else:
                            at[c] = do(ins)
                need(made[0])

            def split_lo(j):
                if j:
                    wait("hi_ready", j)
                name, _ = lo_made(j)
                tell(V.tensor_tensor(lo_part(j), weights(j), plain(hi_part(j)), ALU.subtract), name)

            def split_y(n, y, m_before):
                if m_before is not None:
                    wait("proj_done", UNIT[m_before, 3] + 1)
                tell(V.tensor_copy(src_hi[:, :, :], y), "y_hi")
                wait("y_hi", n)
                tell(V.tensor_tensor(BRANCH_LO[4 - n if n < 4 else 0], y, plain(src_hi[:, :, :]), ALU.subtract), "y_split")

            wait("sq_done", NT)
            tell(V.tensor_scalar(ss, ss, 1.0 / D, EPS, ALU.mult, ALU.add), "ss_ready")
            wait("rs_ready")
            for t in range(NT):
                tell(V.tensor_scalar(xn[:, t, :], x_sb[:, t, :], rs[:, t:t + 1], None, ALU.mult), "xn_ready")
            wait(*front_full(0))
            link(V.tensor_copy(hi_part(0), weights(0)))
            split_lo(0)
            for b in range(4):
                wait("xnT_hi_ready", b + 1)
                for k in range(2 * b, 2 * b + 2):
                    ins = V.scalar_tensor_tensor(xnT_lo[:, k, :], bank[b][:, (k % 2) * SEQ:(k % 2 + 1) * SEQ],
                                                 w_mix[:, k:k + 1], plain(xnT_hi[:, k, :]), ALU.mult, ALU.subtract)
                tell(ins, "xnT_split")
            split_lo(1)
            wait("wab_loaded", 16)
            tell(V.tensor_copy(w_abs_hi[:, :, :], w_abs[:, :, :]), "wab_split")
            wait("wab_split")
            tell(V.tensor_tensor(w_abs_lo[:, :, :], w_abs[:, :, :], plain(w_abs_hi[:, :, :]), ALU.subtract), "wab_split")
            split_lo(2)
            wait("prm_done")
            tell(V.tensor_copy(prm[:, :, 0:NPRM],
                               bank[X0][:, 0:NCH * 52].rearrange("p (c r) -> p c r", c=NCH)[:, :, 0:NPRM]), "prm_taken")
            wait("ws_done")
            tell(V.tensor_copy(wcT[:, :, :], bank4(X1)), "ws_taken")
            wait("prm_taken")
            link(V.tensor_scalar(prm[:, :, RLW:RLB + 1], prm[:, :, RLW:RLB + 1], 0.5, None, ALU.mult))

            wait("ab_done")
            wait("small_loaded", 48)
            ab = bank[Y0][:, 0:NT * 2 * H].rearrange("p (t c) -> p t c", t=NT)
            wait("beta_tanh")
            link(V.tensor_tensor(th(e1), ab[:, :, H:2 * H], rows(dtb, NT), ALU.add))
            tell(V.scalar_tensor_tensor(e2, e1, -1.0, e1, ALU.mult, ALU.max), "abs_ready")
            link(V.tensor_scalar(beta, beta, 0.5, 0.5, ALU.mult, ALU.add))
            tell(V.tensor_scalar(e1, e1, 0.0, None, ALU.max), "ab_taken")
            wait("log_ready")
            wait("ab_taken")
            link(V.tensor_tensor(e1, e1, e3, ALU.add))
            link(V.tensor_tensor(th(e1), th(e1), rows(expA, NT), ALU.mult))
            link(V.tensor_scalar(gl, e1, -1.0, None, ALU.mult))
            wait("xT_done", 4)
            tell(V.tensor_copy(g_wide, gl.rearrange("p (t h) -> p t h", t=NT).unsqueeze(3).to_broadcast([P, NT, H, P])),
                 "g_ready")

            def silu(ch, t2, name):
                wait(name + "_tanh")
                tell(V.scalar_tensor_tensor(ch, t2, 1.0, ch, ALU.add, ALU.mult), name + "_act")

            wait("pads_ready")
            wait("proj_taken_act", 2)
            conv(k_in, k_ch, RK, TAPS, "k_conv")

            wait("gc_done")
            gc = bank[Y1][:, 0:NT * 2 * H].rearrange("p (t c) -> p t c", t=NT)
            link(V.tensor_copy(th(gcum), gc[:, :, 0:H]))
            tell(V.tensor_tensor(th(e2), gc[:, :, H:2 * H], th(gcum), ALU.subtract), "gc_taken")
            wait("rows_done")
            for t in range(NT):
                tell(V.tensor_tensor(decay[:, t], bank4(X0 + t), wide(th(gcum)[:, t, :], P), ALU.subtract), "decay_taken")
            wait("decay_taken", NT)
            tell(V.tensor_tensor(thf(10), thf(10), rows(lo_incl[:, :], NT * H), ALU.mult), "decay_log")
            wait("egc_ready")
            link(V.tensor_tensor(bgk, beta, egc, ALU.mult))
            silu(k_ch, tan[0], "k")

            wait("proj_taken_act", 4)
            conv(q_in, q_ch, RQ, TAPS, "q_conv")

            def norm(name, ssx):
                wait(f"sq{name}_done")
                link(V.tensor_reduce(ssx, squares, AXX, ALU.add))
                tell(V.tensor_scalar(ssx, ssx, 0.25, EPS, ALU.mult, ALU.add), f"ss{name}_ready")

            wait("sqk_done")
            norm("k", ssk)
            silu(q_ch, tan[1], "q")
            wait("rk_ready")
            link(V.tensor_scalar(rk, rk, 0.5, None, ALU.mult))
            for t in range(NT):
                tell(V.tensor_tensor(k_tok[:, t], bank4(Y0 + t), wide(th(rk)[:, t, :], P), ALU.mult), "kn_ready")
            wait("kn_ready", NT)
            tell(V.tensor_tensor(thf(1), thf(0), wide(bgk, P), ALU.mult), "kbg_ready")

            wait("proj_taken_act", 6)
            conv(v_in, v_ch, RV, TAPS, "v_conv")
            norm("q", ssq)
            wait("rq_ready")
            link(V.tensor_scalar(rq, rq, 0.5 * float(P) ** -0.5, None, ALU.mult))
            for t in range(NT):
                tell(V.tensor_tensor(q_tok[:, t], bank4(X0 + t), wide(th(rq)[:, t, :], P), ALU.mult), "qn_ready")
            wait("qn_ready", NT)
            silu(v_ch, tan[0], "v")
            tell(V.tensor_tensor(thf(3), thf(2), wide(egc, P), ALU.mult), "qd_ready")
            link(V.tensor_scalar(e1, beta, 0.5, None, ALU.mult))
            wait("vf_done")
            for t in range(NT):
                tell(V.tensor_tensor(vb_tok[:, t], bank4(X0 + t), wide(th(e1)[:, t, :], P), ALU.mult), "vb_ready")
            wait("kb_done")
            wait("ekd_ready")
            tell(V.tensor_tensor(thf(0), thf(0), wide(ekd, P), ALU.mult), "kd_ready")

            for h in range(2):
                wait("proj_taken_act", bank_free(UNIT[PCG, h])[1])
                a = conf_acc[:, 2 * h:2 * h + 2, :]
                tell(V.scalar_tensor_tensor(conf_pad[:, 2 * h:2 * h + 2, CTAPS - 1:], tan[1][:, 2 * h:2 * h + 2, :], 1.0,
                                            a, ALU.add, ALU.mult), "conf_in")
            conf_parts = [(c0, j) for c0 in (0, 2) for j in range(0, CTAPS, 4)]

            def conf_part():
                if conf_parts:
                    c0, j = conf_parts.pop(0)
                    conv(conf_pad, conf_acc, RC, CTAPS, None, range(c0, c0 + 2), j, min(j + 4, CTAPS))

            wait("conf_in", 2)

            wait("KK_done")
            wait("decay_exp")
            for t in range(NT):
                for h in range(H):
                    tell(V.scalar_tensor_tensor(L_[:, t, h], bank4(Y0 + t)[:, h, :], th(beta)[:, t, h:h + 1],
                                                decay[:, t, h], ALU.mult, ALU.mult), "KK_taken")
            wait("KK_taken", NT * H)
            tell(V.tensor_tensor(thf(11), thf(11), rows(lo_strict[:, :], NT * H), ALU.mult), "L_ready")
            conf_part()
            wait("QK_done")
            for t in range(NT):
                ins = V.tensor_tensor(A_[:, t], bank4(X0 + t), decay[:, t], ALU.mult)
                link(ins) if t == 0 else tell(ins, "A_masked")
            wait("A_masked")
            tell(V.tensor_tensor(thf(13), thf(13), rows(lo_incl[:, :], NT * H), ALU.mult), "A_ready")

            for h in range(2):
                u = UNIT[PSX, h]
                wait("proj_done", u + 1)
                wait("proj_taken_act", bank_free(UNIT[PSC, h])[1])
                tell(V.tensor_tensor(cx[:, 2 * h:2 * h + 2, STAPS - 1:], workA[:, 2 * h:2 * h + 2, :],
                                     bank[u % 4][:, :].rearrange("p (c t) -> p c t", c=2), ALU.mult), "proj_taken_dve")

            wait("LT_taken")
            wait("qdT_ready")
            link(V.tensor_tensor(thf(3), thf(12), rows(merge[:, 0, :], NT * H), ALU.mult))
            link(V.scalar_tensor_tensor(thf(3), thf(3), -1.0, rows(ident[:, :], NT * H), ALU.mult, ALU.add))
            link(V.tensor_tensor(thf(2), thf(11), rows(merge_lo[:, :], NT * H), ALU.mult))
            tell(V.scalar_tensor_tensor(thf(2), thf(2), -1.0, rows(ident[:, :], NT * H), ALU.mult, ALU.add), "T_ready")

            def merge_mask(n):
                wait("T_ready", 1)
                if n > 1:
                    wait("U_done", n - 1)
                tell(V.tensor_tensor(thf(11), thf(12), rows(merge[:, n, :], NT * H), ALU.mult), "QM_ready")

            def merge_take(n):
                if n < NM - 1:
                    wait("TU_done", n)
                wait("TUt_done", n)
                for t in range(NT):
                    if n < NM - 1:
                        last = V.tensor_tensor(T_[:, t], T_[:, t], bank4(X0 + t), ALU.subtract)
                        tell(last, "T_ready") if t else do(last)
                for t in range(NT):
                    last = V.tensor_tensor(V_[:, t], V_[:, t], bank4(Y0 + t), ALU.subtract)
                    tell(last, "W_taken") if t else do(last)

            def sc_out(h):
                u = UNIT[PSB, h]
                wait("proj_done", u + 1)
                w = workA[:, 2 * h:2 * h + 2, :]
                tell(V.tensor_tensor(w, w, bank[u % 4][:, :].rearrange("p (c t) -> p c t", c=2), ALU.mult),
                     "proj_taken_dve")

            def branch_unit(m, q):
                u = UNIT[m, q]
                c = 2 * (q % 2)
                wait("proj_taken_act", bank_free(UNIT[GATES[m] + q // 2, q % 2])[1])
                wait("proj_done", u + 1)
                g = tan[q // 2][:, c:c + 2, :]
                o = merged[:, q // 2, c:c + 2, :]
                ps = bank[u % 4][:, :].rearrange("p (c t) -> p c t", c=2)
                if m == PW3:
                    tell(V.scalar_tensor_tensor(o, g, 1.0, ps, ALU.add, ALU.mult), "proj_taken_dve")
                else:
                    tell(V.scalar_tensor_tensor(g, g, 1.0, ps, ALU.add, ALU.mult), "proj_taken_dve")
                    wait("proj_taken_dve", bank_free(u)[1])
                    tell(V.tensor_tensor(o, o, g, ALU.add), "gate_used")

            GATES = {PW3: PG3A, PW2: PG2A, PW1: PG1A, PW0: PG0A}

            merge_mask(1)
            link(V.memset(cx[:, :, 0:STAPS - 1], 0.0))
            wait("proj_taken_dve", 2)
            conv(cx, workA, RS, STAPS)
            sc_out(0)
            sc_out(1)
            wait("proj_taken_dve", bank_free(UNIT[PSB, 1])[1])
            split_y(1, workA, None)
            merge_take(1)
            merge_mask(2)
            conf_part()
            conf_part()
            merge_take(2)
            merge_mask(3)
            conf_part()
            conf_part()
            merge_take(3)
            merge_mask(4)
            for q in range(4):
                branch_unit(PW3, q)
                if q % 2:
                    conf_part()
            merge_take(4)
            merge_mask(5)

            GC = 0.7978845608028654

            def gelu_unit(n, m, h, dst):
                u = UNIT[m, h]
                ps = bank[u % 4][:, :]
                s = blk(16 + n // 2)[:, (n % 2) * 512:(n % 2 + 1) * 512]
                wait("gelu_sq", n + 1)
                link(V.tensor_scalar(s, s, 0.044715, 1.0, ALU.mult, ALU.add))
                tell(V.tensor_tensor(s, s, ps, ALU.mult), "gelu_in")
                wait("gelu_tanh", n + 1)
                tell(V.scalar_tensor_tensor(dst, s, 1.0, ps, ALU.add, ALU.mult), "proj_taken_dve")

            def layer_stats(src, t):
                link(V.bn_stats(bnst[:, 6 * t:6 * t + 6], src))
                link(V.bn_aggr(mv[:, 2 * t:2 * t + 2], bnst[:, 6 * t:6 * t + 6]))

            for t in range(NT):
                gelu_unit(t, PGV, t, gm_v[:, t, :])
                wait("proj_taken_dve", bank_free(UNIT[PGV, t])[1])
                layer_stats(gm_v[:, t, :], t)
            merge_take(5)
            mvv = mv.rearrange("p (t c) -> p t c", t=NT)
            tell(V.tensor_scalar(rv, mvv[:, :, 1], 4 * EPS, None, ALU.add), "gm_var")
            conf_part()
            wait("gm_rstd")
            for t in range(NT):
                do(V.tensor_scalar(gm_v[:, t, :], gm_v[:, t, :], mvv[:, t, 0:1], rv[:, t:t + 1],
                                   ALU.subtract, ALU.mult))
            need(made[0])
            wait("lnrows_loaded", 32)
            link(V.tensor_tensor(gm_v, gm_v, rows(ln_rows[:, 0, :], NT), ALU.mult))
            tell(V.tensor_tensor(gm_v, gm_v, rows(ln_rows[:, 1, :], NT), ALU.add), "gm_ln")
            for h in range(2):
                gelu_unit(NT + h, PGU, h, gm_u[:, 2 * h:2 * h + 2, :].rearrange("p c t -> p (c t)"))

            def chunk_new(c):
                t, b = divmod(c, P // CH)
                r = slice(b * CH, (b + 1) * CH)
                if c == 0:
                    wait("u_taken")
                    tell(V.tensor_copy(vn_tok[r, t], u_tok[r, t]), "vn_ready")
                else:
                    wait("ws_state", c)
                    tell(V.tensor_tensor(vn_tok[r, t], u_tok[r, t], bank4(X0 + t)[r], ALU.subtract), "vn_ready")

            def chunk_state(c):
                wait("state_add", c + 1)
                if c == 0:
                    tell(V.tensor_copy(state[:, :, :], bank4(Y1)), "state_ready")
                else:
                    wait("ws_state", c)
                    wait("o_done", c + 1)
                    link(V.tensor_tensor(state[:, :, :], state[:, :, :],
                                         wide(egl.rearrange("p (t h b) -> p t h b", t=NT, h=H)[:, c // 2, :, c % 2], P),
                                         ALU.mult))
                    tell(V.tensor_tensor(state[:, :, :], state[:, :, :], bank4(Y1), ALU.add), "state_ready")

            wait("U_done", NM - 1)
            chunk_new(0)
            conf_part()
            chunk_state(0)
            wait("mix_done")
            wait("bs_loaded", 16)
            wait("proj_taken_dve", bank_free(UNIT[PGU, 1])[1])
            for n in range(2):
                v = tan[1].rearrange("p (n g) (t i) -> p n g t i", n=2, t=NT)
                for g in range(2):
                    tell(V.tensor_tensor(v[:, n, g], bank[X0 + n][:, g * SEQ:(g + 1) * SEQ].rearrange("p (t i) -> p t i", t=NT),
                                       rows(bs_row[:, 2 * n + g, :], NT), ALU.add), "mix_taken")
            wait("mix_taken", NCH)
            tell(V.scalar_tensor_tensor(workB, tan[1], 0.5, gm_u, ALU.mult, ALU.mult), "y2_ready")
            wait("y2_ready")
            split_y(2, workB, PW3)
            chunk_new(1)
            conf_part()
            chunk_state(1)
            conf_part()
            chunk_new(2)
            for q in range(4):
                branch_unit(PW2, q)
                if q < 3:
                    conf_part()
            chunk_state(2)
            while len(conf_parts) > 0:
                conf_part()
            for c in range(NCH):
                tell(V.tensor_scalar(conf_acc[:, c, :], conf_acc[:, c, :], 0.5, prm[:, c, RCB:RCB + 1],
                                     ALU.mult, ALU.add), "cf_conv")
            chunk_new(3)
            for h in range(2):
                u = UNIT[PZ, h]
                z = zbuf[:, 2 * h:2 * h + 2, :]
                wait("z_tanh", h + 1)
                tell(V.scalar_tensor_tensor(z, z, 1.0, bank[u % 4][:, :].rearrange("p (c t) -> p c t", c=2),
                                            ALU.add, ALU.mult), "proj_taken_dve")
            wait("sqo_done")
            link(V.tensor_reduce(sso, squares, AXX, ALU.add))
            tell(V.tensor_scalar(sso, sso, 1.0 / P, EPS, ALU.mult, ALU.add), "sso_ready")
            wait("cfT_done")
            for t in range(NT):
                layer_stats(bank[Y0 + t][:, :], t)
            tell(V.tensor_scalar(rv, mvv[:, :, 1], EPS, None, ALU.add), "cf_var")
            wait("ro_ready")
            tell(V.tensor_tensor(thf(10), thf(10), wide(ro, P), ALU.mult), "on_ready")
            wait("cf_rstd")
            wait("proj_done", UNIT[PW2, 3] + 1)
            for t in range(NT):
                tell(V.tensor_scalar(cf_tok[:, t].rearrange("p c d -> p (c d)"), bank[Y0 + t][:, :], mvv[:, t, 0:1],
                                     rv[:, t:t + 1], ALU.subtract, ALU.mult), "cf_norm")
            wait("cf_tanh", 2)
            tell(V.scalar_tensor_tensor(conf_acc, cf_tok.rearrange("p t h d -> p (t h d)").rearrange("p (c t) -> p c t", c=NCH),
                                        1.0, conf_acc, ALU.add, ALU.mult), "y1_ready")
            wait("y1_ready")
            split_y(3, conf_acc, PW2)
            wait("oT_done")
            link(V.tensor_scalar(w_gn, w_gn, 0.5, None, ALU.mult))
            wait("proj_taken_dve", bank_free(UNIT[PZ, 1])[1])
            for n in range(2):
                last = V.scalar_tensor_tensor(workA[:, 2 * n:2 * n + 2, :].rearrange("p c t -> p (c t)"), bank[X0 + n][:, :],
                                              w_gn, zbuf[:, 2 * n:2 * n + 2, :].rearrange("p c t -> p (c t)"),
                                              ALU.mult, ALU.mult)
                tell(last, "y0_ready") if n else do(last)
            for q in range(4):
                branch_unit(PW1, q)
            wait("y0_ready")
            split_y(4, workA, PW1)
            for q in range(4):
                branch_unit(PW0, q)
                wait("gate_used", 8 + q + 1)
                part = merged[:, q // 2, 2 * (q % 2):2 * (q % 2) + 2, :]
                hi = merged_hi[:, 2 * q:2 * q + 2, :]
                tell(V.tensor_copy(hi, part), "merged_hi_ready")
                wait("merged_hi_ready", q + 1)
                tell(V.tensor_tensor(merged_lo[:, q // 2, 2 * (q % 2):2 * (q % 2) + 2, :], part, plain(hi),
                                     ALU.subtract), "merged_split")
            wait("xres_loaded", 32)
            for n, m in enumerate((PO0, PO1)):
                for t in range(NT):
                    u = UNIT[m, t]
                    wait("proj_done", u + 1)
                    o = x2[:, t, n * BW:(n + 1) * BW]
                    tell(V.scalar_tensor_tensor(o, bank[u % 4][:, :], 0.5, o, ALU.mult, ALU.add), "proj_taken_dve")

            do(V.memset(conf_pad[:, 2, 0:P // 2], 0.0))
            link(V.memset(conf_pad[:, 3, 0:BW // 2], 0.0))
            for t in range(NT):
                wait("sq2_done", t + 1)
                tell(V.tensor_scalar(ss[:, t:t + 1], ss[:, t:t + 1], 1.0 / D, EPS, ALU.mult, ALU.add), "ss2_ready")
            wait("moew_loaded", 16)
            for t in range(NT):
                wait("rs2_ready", t + 1)
                tell(V.scalar_tensor_tensor(xm[:, t, :].rearrange("p (k q) -> p q k", k=KC),
                                            x2[:, t, :].rearrange("p (q k) -> p q k", k=KC), rs[:, t:t + 1],
                                            moe_w.rearrange("p (q k) -> p q k", k=KC), ALU.mult, ALU.mult), "xm_ready")
            for t in range(NT):
                wait("xmT_done", t + 1)
                tell(V.tensor_copy(xmT[:, 1, :, t * P:(t + 1) * P], bank4(X1 + 2 * t)), "xmT_dve")
            wait("masks_ready")
            grp_max, grp_idx, in_grp, sel, exp_max, exp_idx, in_1st, in_2nd, share, both, w_exp = (
                r8[:, n] for n in range(11))

            def by_group(v):
                return v.unsqueeze(2).to_broadcast([P, NT, NG, EG])

            def along(v, n=8):
                return v.to_broadcast([P, NT, n])

            iota_t = rows(iota_s[:, 0:8], NT)
            wait("logits_done", NT)
            link(V.tensor_copy(lg, bank[X0][:, 0:NT * (NG + NE)].rearrange("p (t e) -> p t e", t=NT)))
            for t in range(NT):
                do(V.max(grp_max[:, t], lg[:, t, 0:NG]))
            need(made[0])
            for t in range(NT):
                do(V.max_index(best_index[:, 0, t], grp_max[:, t], lg[:, t, 0:NG]))
            tell(V.tensor_scalar(share[:, :, 0:1], grp_max[:, :, 0:1], -1.0, None, ALU.mult), "ngmax_ready")
            need(made[0])
            link(V.tensor_copy(grp_idx, best_index[:, 0]))
            link(V.tensor_tensor(in_grp, iota_t, along(grp_idx[:, :, 0:1]), ALU.is_equal))
            group_of = in_grp.unsqueeze(3).to_broadcast([P, NT, NG, EG])
            link(V.tensor_tensor(tmp64.rearrange("p t (g e) -> p t g e", g=NG),
                                 lg[:, :, NG:].rearrange("p t (g e) -> p t g e", g=NG), group_of, ALU.mult))
            link(V.tensor_reduce(sel, tmp64.rearrange("p t (g e) -> p t e g", g=NG), AXX, ALU.add))
            for t in range(NT):
                do(V.max(exp_max[:, t], sel[:, t]))
            need(made[0])
            tell(V.tensor_tensor(share[:, :, 2:3], exp_max[:, :, 1:2], exp_max[:, :, 0:1], ALU.subtract), "gap_ready")
            for t in range(NT):
                do(V.max_index(best_index[:, 1, t], exp_max[:, t], sel[:, t]))
            need(made[0])
            link(V.tensor_copy(exp_idx, best_index[:, 1]))
            do(V.tensor_tensor(in_1st, iota_t, along(exp_idx[:, :, 0:1]), ALU.is_equal))
            link(V.tensor_tensor(in_2nd, iota_t, along(exp_idx[:, :, 1:2]), ALU.is_equal))
            link(V.tensor_tensor(both, in_1st, in_2nd, ALU.add))
            tell(V.tensor_tensor(assigned.rearrange("p t (g e) -> p t g e", g=NG), group_of, by_group(both), ALU.mult),
                 "assigned_ready")
            wait("exps_done")
            link(V.scalar_tensor_tensor(share[:, :, 4:5], share[:, :, 3:4], 1.0, share[:, :, 1:2], ALU.add, ALU.mult))
            link(V.reciprocal(share[:, :, 5:6], share[:, :, 4:5]))
            do(V.tensor_tensor(share[:, :, 6:7], share[:, :, 5:6], share[:, :, 3:4], ALU.mult))
            link(V.tensor_tensor(in_1st, in_1st, along(share[:, :, 5:6]), ALU.mult))
            link(V.tensor_tensor(in_2nd, in_2nd, along(share[:, :, 6:7]), ALU.mult))
            link(V.tensor_tensor(w_exp, in_1st, in_2nd, ALU.add))
            do(V.tensor_tensor(weight.rearrange("p t (g e) -> p t g e", g=NG), group_of, by_group(w_exp), ALU.mult))
            wait("counts_done")
            wait("assigned_ready")
            link(V.scalar_tensor_tensor(slot, bank[Y0][:, 0:NT * NE].rearrange("p (t e) -> p t e", t=NT), 1.0,
                                        assigned, ALU.add, ALU.mult))
            link(V.tensor_scalar(slot, slot, -1.0, None, ALU.add))
            link(V.tensor_reduce(npass_f[:, 0:1], bank[Y1][:, 0:NE], AXX, ALU.max))
            full = r8[:, 12, 0]
            link(V.tensor_scalar(full, iota_s[:, 0:8], float(SL), None, ALU.mult))
            link(V.tensor_scalar(full, full, npass_f[:, 0:1], None, ALU.is_lt))
            link(V.tensor_reduce(npass_f[:, 1:2], full, AXX, ALU.add))
            tell(V.tensor_copy(npass_i[:, 0:1], npass_f[:, 1:2]), "npass_ready")

            wait("npass_ready")
            dve.sem_inc(S["y_taken_dve"], 1)
            n = dve.value_load(npass_i[0:1, 0:1], min_val=1, max_val=SEQ // SL)
            with dve.Fori(0, n) as ps:
                with dve.Fori(0, NP) as bp:
                    for half in range(UB):
                        b = bp * UB + half
                        it = ps * NB + b
                        wait("xg_done", it * 2 + 1)
                        e4 = bass.ds(b * EB, EB)
                        sl = slot[:, :, e4].unsqueeze(3).to_broadcast([P, NT, EB, SL])
                        io = iota_s[:, :].unsqueeze(1).unsqueeze(1).to_broadcast([P, NT, EB, SL])
                        V.tensor_tensor(onehot, sl, io, ALU.is_equal).then_inc(S["onehot_ready"], 1)
                        wait("onehot_ready", it + 1)
                        wait("scatter_done", it + 1)
                        V.tensor_tensor(onehot_w, onehot, weight[:, :, e4].unsqueeze(3).to_broadcast([P, NT, EB, SL]),
                                        ALU.mult).then_inc(S["onehot_w_ready"], 1)
                        wait("xg_done", it * 2 + 3)
                        V.tensor_copy(xgT[:, HK:KC, :], bank4(Y1)).then_inc(S["xg_taken_dve"], 1)
                        wait("scatter_done", it + 2)
                        wait("summed", it + 1)
                        V.tensor_copy(scatter, bank[X0][:, 0:NT * P]).then_inc(S["scatter_taken"], 1)
                        wait("gate_tanh2", it + 1)
                        V.scalar_tensor_tensor(gate_t, gate_t, 1.0, bank[X0][:, :], ALU.add, ALU.mult).then_inc(S["gated"], 1)
                        wait("gated", it + 1)
                        wait("ring_free", it * PB + 2 * HK)
                        V.scalar_tensor_tensor(hid, gate_t, 0.5, bank[X1][:, :], ALU.mult, ALU.mult).then_inc(S["hid_ready"], 1)
                        wait("ring_free", it * PB + PB)
                        V.tensor_copy(y_sb[:, BW:2 * BW], bank[Y1][:, :]).then_inc(S["y_taken_dve"], 1)
                V.tensor_scalar(slot, slot, float(-SL), None, ALU.add).then_inc(S["slots_moved"], 1)
                wait("slots_moved", ps + 1)

            wait("sq3_done", 1)
            link(V.tensor_tensor(ss, e2[:, 0:2], e2[:, 2:4], ALU.add))
            tell(V.tensor_scalar(ss, ss, 1.0 / D, EPS, ALU.mult, ALU.add), "ss3_ready")
            wait("finw_loaded", 16)
            wait("rs3_ready")
            for t in range(NT):
                for n2 in range(2):
                    V.scalar_tensor_tensor(y_out[:, t, n2 * BW:(n2 + 1) * BW], acc[t][n2][:, :], rs[:, t:t + 1],
                                           fin_w[:, n2 * BW:(n2 + 1) * BW], ALU.mult, ALU.mult).then_inc(S["out_ready"], 1)

        @block.scalar
        def _(act):
            A = nc.scalar.activation

            def load(dst, src, name):
                act.dma_start(dst, src).then_inc(S[name], 16)

            def wait(name, n=1):
                act.wait_ge(*S.at(name, n))

            def tell(ins, name):
                ins.then_inc(S[name], 1)

            load(w_mix[:, :], mix_norm_w[0].rearrange("(p k) -> p k", k=KC), "mix_loaded")
            load(w_abs[:, :, :], w_in[0, :, OAB:OAB + 2 * H].rearrange("(p k) n -> p k n", k=KC), "wab_loaded")
            load(alog, gdn_A_log.to_broadcast([P, H]), "small_loaded")
            load(dtb, gdn_dt_bias.to_broadcast([P, H]), "small_loaded")
            load(w_gn, gdn_norm_w[0].rearrange("(p a) -> p a", a=1), "small_loaded")
            for t in range(NT):
                wait(f"x_loaded{t}", 16)
                tell(A(xn[:, t, :], x_sb[:, t, :], ACT.Square, accum_out=ss[:, t:t + 1]), "sq_done")
            wait("small_loaded", 48)
            tell(A(expA, alog, ACT.Exp), "expA_ready")
            wait("mix_loaded", 16)
            for b in range(4):
                wait("xT_done", b + 1)
                for k in range(2 * b, 2 * b + 2):
                    ins = A(xnT_hi[:, k, :], bank[b][:, (k % 2) * SEQ:(k % 2 + 1) * SEQ], ACT.Copy,
                            scale=w_mix[:, k:k + 1])
                tell(ins, "xnT_hi_ready")
            jobs = list(range(1, NJ))

            def split_hi(unit=None):
                while jobs and (jobs[0] < NHI or unit and jobs[0] - NHI < jobs_by(unit)):
                    j = jobs.pop(0)
                    wait(*front_full(j // 2))
                    if j >= NHI:
                        wait(*job_used(j - NHI))
                    tell(A(hi_part(j), weights(j), ACT.Copy), "hi_ready")

            split_hi()
            wait("ab_done")
            ab = bank[Y0][:, 0:NT * 2 * H].rearrange("p (t c) -> p t c", t=NT)
            tell(A(th(beta), ab[:, :, 0:H], ACT.Tanh, scale=0.5), "beta_tanh")
            wait("abs_ready")
            tell(A(e3, e2, ACT.Exp, scale=-1.0), "exp_abs")
            wait("exp_abs")
            tell(A(e3, e3, ACT.Ln, bias=1.0), "log_ready")

            def copy_unit(m, h, dst):
                u = UNIT[m, h]
                wait("proj_done", u + 1)
                tell(A(dst, bank[u % 4][:, :].rearrange("p (c t) -> p c t", c=2), ACT.Copy), "proj_taken_act")
                split_hi((m, h))

            wait("pads_ready")
            for h in range(2):
                copy_unit(PK, h, k_in[:, 2 * h:2 * h + 2, TAPS - 1:])
            wait("gc_taken")
            tell(A(egc, gcum, ACT.Exp), "egc_ready")
            wait("k_conv")
            tell(A(tan[0], k_ch, ACT.Tanh, scale=0.5), "k_tanh")
            wait("decay_taken", NT)
            for t in range(NT):
                v = egl.rearrange("p (t h b) -> p t h b", t=NT, h=H)[:, t]
                ins = A(v, bank4(X0 + t)[:, :, CH - 1::CH], ACT.Exp)
                if t:
                    tell(ins, "egl_ready")
            wait("gc_taken")
            tell(A(ekd, e2, ACT.Exp), "ekd_ready")
            for h in range(2):
                copy_unit(PQ, h, q_in[:, 2 * h:2 * h + 2, TAPS - 1:])
            wait("decay_log")
            tell(A(thf(10), thf(10), ACT.Exp, scale=-1.0), "decay_exp")
            wait("kf_done")
            for t in range(NT):
                ins = A(squares[:, t * H:(t + 1) * H, :], bank4(Y0 + t), ACT.Square)
                if t:
                    tell(ins, "sqk_done")
            copy_unit(PV, 0, v_in[:, 0:2, TAPS - 1:])
            wait("q_conv")
            wait("rows_done")
            tell(A(tan[1], q_ch, ACT.Tanh, scale=0.5), "q_tanh")
            copy_unit(PV, 1, v_in[:, 2:4, TAPS - 1:])
            wait("qf_done")
            wait("ssk_ready")
            for t in range(NT):
                ins = A(squares[:, t * H:(t + 1) * H, :], bank4(X0 + t), ACT.Square)
                if t:
                    tell(ins, "sqq_done")
            wait("v_conv")
            wait("k_act")
            tell(A(tan[0], v_ch, ACT.Tanh, scale=0.5), "v_tanh")
            copy_unit(PCA, 0, conf_acc[:, 0:2, :])

            def take(done, dst0, dst, src, name):
                wait(*done)
                for t in range(NT):
                    ins = A(dst[:, t], bank4(src + t), ACT.Copy)
                    if t:
                        tell(ins, name)

            take(("kb_done", 1), 0, kT, Y0, "kT_ready")
            copy_unit(PCA, 1, conf_acc[:, 2:4, :])

            wait("q_act")
            for h in range(2):
                u = UNIT[PCG, h]
                wait("proj_done", u + 1)
                A(tan[1][:, 2 * h:2 * h + 2, :], bank[u % 4][:, :].rearrange("p (c t) -> p c t", c=2), ACT.Tanh,
                  scale=0.5).then_inc(S["proj_taken_act"], 1)
                split_hi((PCG, h))
            take(("qb_done", 1), 0, qT, X0, "qT_ready")
            copy_unit(PSC, 0, workA[:, 0:2, :])
            take(("qdb_done", 1), 0, qdT, Y0, "qdT_ready")
            copy_unit(PSC, 1, workA[:, 2:4, :])
            take(("LT_done", 1), 0, Q_, Y0, "LT_taken")
            split_hi((PSX, 0))
            take(("AT_done", 1), 0, AT, X0, "AT_taken")
            split_hi((PSX, 1))
            load(ln_rows[:, 0, :], gmlp_ln_w.to_broadcast([P, BW]), "lnrows_loaded")
            load(ln_rows[:, 1, :], gmlp_ln_b.to_broadcast([P, BW]), "lnrows_loaded")

            def gate_unit(bi, g, h):
                m = (PG3A, PG2A, PG1A, PG0A)[bi] + g
                if bi > 1:
                    wait("gate_used", 4 * (bi - 2) + 2 * g + h + 1)
                u = UNIT[m, h]
                wait("proj_done", u + 1)
                A(tan[g][:, 2 * h:2 * h + 2, :], bank[u % 4][:, :].rearrange("p (c t) -> p c t", c=2), ACT.Tanh,
                  scale=0.5).then_inc(S["proj_taken_act"], 1)
                split_hi((m, h))

            def take_u(n):
                take(("U_done", n), 0, U_, Y0, "U_taken")

            take_u(1)
            split_hi((PSB, 1))
            wait("v_act")
            wait("conf_in", 2)
            gate_unit(0, 0, 0)
            take_u(2)
            gate_unit(0, 0, 1)
            gate_unit(0, 1, 0)
            take_u(3)
            gate_unit(0, 1, 1)
            take_u(4)
            split_hi((PW3, 3))

            def gelu_act(n, m, h):
                u = UNIT[m, h]
                s = blk(16 + n // 2)[:, (n % 2) * 512:(n % 2 + 1) * 512]
                wait("proj_done", u + 1)
                if n == 0:
                    wait("proj_taken_dve", bank_free(UNIT[PW3, 3])[1])
                tell(A(s, bank[u % 4][:, :], ACT.Square), "gelu_sq")
                wait("gelu_in", n + 1)
                tell(A(s, s, ACT.Tanh, scale=0.7978845608028654), "gelu_tanh")
                split_hi((m, h))

            gelu_act(0, PGV, 0)
            take_u(5)
            gelu_act(1, PGV, 1)
            wait("TUt_done", NM - 1)
            load(bs_row, gmlp_b_s[0].rearrange("g i -> (g i)").rearrange("(a n) -> a n", a=1).to_broadcast([P, BW]), "bs_loaded")
            gelu_act(2, PGU, 0)
            gelu_act(3, PGU, 1)
            take(("u_done", 1), 0, u_tok, X0, "u_taken")
            wait("gm_ln")
            take(("wT_done", 1), 0, wT, Y0, "wT_taken")
            for t in range(NT):
                load(x_res[:, t, :], x[0, t * P:(t + 1) * P, :], "xres_loaded")

            def take_o(c):
                t, b = divmod(c, P // CH)
                r = slice(b * CH, (b + 1) * CH)
                wait("o_done", c + 1)
                tell(A(o_tok[r, t], bank4(Y0)[r], ACT.Copy), "o_taken")

            take_o(0)
            wait("proj_taken_dve", bank_free(UNIT[PGU, 0])[1])
            gate_unit(1, 0, 0)
            wait("proj_taken_dve", bank_free(UNIT[PGU, 1])[1])
            gate_unit(1, 0, 1)
            take_o(1)
            wait("y2_ready")
            gate_unit(1, 1, 0)
            gate_unit(1, 1, 1)
            split_hi((PW2, 1))
            take_o(2)
            split_hi((PW2, 3))
            for h in range(2):
                u = UNIT[PZ, h]
                wait("proj_done", u + 1)
                tell(A(zbuf[:, 2 * h:2 * h + 2, :], bank[u % 4][:, :].rearrange("p (c t) -> p c t", c=2), ACT.Tanh,
                       scale=0.5), "z_tanh")
                split_hi((PZ, h))
            take_o(3)
            wait("o_taken", 4)
            tell(A(squares, thf(10), ACT.Square), "sqo_done")
            gate_unit(2, 0, 0)
            gate_unit(2, 0, 1)
            wait("cfB_done")
            for c in range(NCH):
                ins = A(conf_acc[:, c, :], bank[Y0 + c // 2][:, (c % 2) * SEQ:(c % 2 + 1) * SEQ], ACT.Identity,
                        bias=prm[:, c, RLB:RLB + 1], scale=prm[:, c, RLW:RLW + 1])
            tell(ins, "cf_tanh")
            wait("cf_tanh", 1)
            tell(A(cf_tok.rearrange("p t h d -> p (t h d)"), conf_acc.rearrange("p c t -> p (c t)"), ACT.Tanh), "cf_tanh")
            gate_unit(2, 1, 0)
            gate_unit(2, 1, 1)
            split_hi((PW1, 1))
            split_hi((PW1, 3))
            for g in range(2):
                for h in range(2):
                    gate_unit(3, g, h)
            split_hi((PW0, 1))
            split_hi((PW0, 3))
            wait("gate_used", 12)
            load(moe_w, moe_norm_w.to_broadcast([P, D]), "moew_loaded")
            load(w_rt[:, :, 0:NG], router_grp[0].rearrange("(p k) e -> p k e", k=KC), "rt_loaded")
            load(w_rt[:, :, NG:], router_exp[0].rearrange("(p k) e -> p k e", k=KC), "rt_loaded")
            split_hi((PO0, 1))
            load(fin_w, final_norm_w.rearrange("(a n) -> a n", a=1).to_broadcast([P, D]), "finw_loaded")

            for t in range(NT):
                wait("proj_taken_dve", bank_free(UNIT[PO1, t])[1])
                tell(A(sq_out[:, t, :], x2[:, t, :], ACT.Square, accum_out=ss[:, t:t + 1]), "sq2_done")
            for t in range(NT):
                wait("xmT_done", t + 1)
                tell(A(xmT[:, 0, :, t * P:(t + 1) * P], bank4(X0 + 2 * t), ACT.Copy), "xmT_act")
            share = r8[:, 8]
            wait("ngmax_ready")
            for t in range(NT):
                A(grp_exp[:, t, :], lg[:, t, 0:NG], ACT.Exp, bias=share[:, t, 0:1], accum_out=share[:, t, 1:2])
            wait("gap_ready")
            tell(A(share[:, :, 3:4], share[:, :, 2:3], ACT.Exp), "exps_done")

            wait("npass_ready")
            act.sem_inc(S["y_taken_act"], 1)
            act.sem_inc(S["hidT_taken"], 1)
            n = act.value_load(npass_i[0:1, 0:1], min_val=1, max_val=SEQ // SL)
            with act.Fori(0, n) as ps:
                with act.Fori(0, NP) as bp:
                    for half in range(UB):
                        b = bp * UB + half
                        it = ps * NB + b
                        wait("xg_done", it * 2 + 2)
                        A(xgT[:, 0:HK, :], bank4(Y0), ACT.Copy).then_inc(S["xg_taken_act"], 1)
                        wait("ring_free", it * PB + 2 * HK - 1)
                        A(gate_t, bank[X0][:, :], ACT.Tanh, scale=0.5).then_inc(S["gate_tanh2"], 1)
                        wait("hidT_done", it + 1)
                        A(hidT, bank4(X0), ACT.Copy).then_inc(S["hidT_taken"], 1)
                        wait("y_half_done", it + 1)
                        wait("summed", it + 1)
                        A(y_sb[:, 0:BW], bank[Y0][:, :], ACT.Copy).then_inc(S["y_taken_act"], 1)

            wait("sum_closed")
            for t in range(NT):
                for n2 in range(2):
                    ins = A(y_out[:, t, n2 * BW:(n2 + 1) * BW], acc[t][n2][:, :], ACT.Square,
                            accum_out=e2[:, t + NT * n2:t + NT * n2 + 1])
            tell(ins, "sq3_done")
            for t in range(NT):
                wait("out_ready", 2 * t + 2)
                act.dma_start(out[0, t * P:(t + 1) * P, :], y_out[:, t, :]).then_inc(S["out_stored"], 16)
            act.wait_ge(*S.at("out_stored", 16 * NT))


_INS = ['x', 'mix_norm_w', 'w_in', 'gdn_conv_w', 'gdn_A_log', 'gdn_dt_bias', 'gdn_norm_w', 'conf_conv_w',
        'conf_conv_b', 'conf_ln_w', 'conf_ln_b', 'gmlp_ln_w', 'gmlp_ln_b', 'gmlp_w_s', 'gmlp_b_s', 'sc_conv_w',
        'w_branch', 'w_out', 'moe_norm_w', 'router_grp', 'router_exp', 'w_gate', 'w_up', 'w_down', 'final_norm_w']


def kernel(**inputs):
    import numpy as _np
    import concourse.bacc as _bacc
    from concourse.bass_utils import run_bass_kernel_spmd as _run

    nc = _bacc.Bacc("TRN2", target_bir_lowering=False, num_devices=1)
    arrays, args = {}, []
    for name in _INS:
        a = _np.ascontiguousarray(inputs[name])
        arrays[f"in_{name}"] = a
        args.append(nc.dram_tensor(f"in_{name}", a.shape, mybir.dt.from_np(a.dtype), kind="ExternalInput").ap())
    out = nc.dram_tensor("out_x", inputs["x"].shape, mybir.dt.float32, kind="ExternalOutput").ap()
    hybrid_trunk_kernel(nc, *args, out)
    r = _run(nc, [arrays], core_ids=[0])
    return r.results[0]["out_x"]
```
